# Optimizing a Trainium2 kernel written in Bass

```python
import jax, jax.numpy as jnp
from jax import lax
import numpy as np
import math

D_MODEL = 1024
BATCH = 1
SEQ = 256
DEPTH = 1

CHUNK = 64
EPS = 1e-6
N_BRANCH = 2
CONV_DIM = D_MODEL
CONV_WIDTH = 3
SSM_EXPAND = 2
D_SSM = SSM_EXPAND * D_MODEL
SSM_HEAD_DIM = 64
SSM_HEADS = D_SSM // SSM_HEAD_DIM
SSM_GROUPS = 8
SSM_STATE = 128
SSM_CONV_WIDTH = 4
SSM_CONV_DIM = D_SSM + 2 * SSM_GROUPS * SSM_STATE
DT_MIN = 1e-3
DT_MAX = 1e-1
D_FF = 4 * D_MODEL
N_MOD = 6


def proj_sizes():
    return (N_BRANCH * D_MODEL,
            CONV_DIM, CONV_DIM, CONV_DIM,
            D_SSM,
            SSM_CONV_DIM,
            SSM_HEADS)

def rms_norm(x, w):
    xf = x.astype(jnp.float32)
    y = xf * lax.rsqrt(jnp.mean(xf * xf, axis=-1, keepdims=True) + EPS)
    return (y * w.astype(jnp.float32)).astype(x.dtype)

def causal_depthwise_conv(x, w):
    k = w.shape[0]
    return lax.conv_general_dilated(
        x, w[:, None, :].astype(x.dtype), window_strides=(1,), padding=((k - 1, 0),),
        dimension_numbers=('NWC', 'WIO', 'NWC'), feature_group_count=x.shape[-1])

def ssd_scan(x, a, b, c):
    bsz, seqlen, h, p = x.shape
    g, n = b.shape[-2:]
    r = h // g
    nc = seqlen // CHUNK

    def to_chunks(t):
        return jnp.moveaxis(t.reshape(bsz, nc, CHUNK, *t.shape[2:]), 1, 0)

    xs = (to_chunks(x.reshape(bsz, seqlen, g, r, p)),
          to_chunks(a.reshape(bsz, seqlen, g, r)),
          to_chunks(b), to_chunks(c))
    tril = jnp.tril(jnp.ones((CHUNK, CHUNK), dtype=bool))[None, :, :, None, None]

    def step(state, inp):
        xq, aq, bq, cq = inp
        a_cum = jnp.cumsum(aq, axis=1)
        seg = a_cum[:, :, None] - a_cum[:, None, :]
        decay = jnp.exp(jnp.where(tril, seg, -jnp.inf))
        scores = jnp.einsum('btgn,bsgn->btsg', cq, bq)
        y_diag = jnp.einsum('btsg,btsgr,bsgrp->btgrp', scores, decay, xq)
        y_off = jnp.einsum('btgn,bgrpn->btgrp', cq, state) * jnp.exp(a_cum)[..., None]
        to_end = jnp.exp(a_cum[:, -1:] - a_cum)
        new_state = (state * jnp.exp(a_cum[:, -1])[..., None, None]
                     + jnp.einsum('bsgn,bsgr,bsgrp->bgrpn', bq, to_end, xq))
        return new_state, y_diag + y_off

    state0 = jnp.zeros((bsz, g, r, p, n), jnp.float32)
    _, y = lax.scan(step, state0, xs)
    return jnp.moveaxis(y, 0, 1).reshape(bsz, seqlen, h, p)

def mixer_sublayer(u, w_in, conv_w, ssm_conv_w, ssm_conv_b, dt_bias, a_log, d_skip,
                   ssm_norm_w, w_conv_out, w_ssm_out, w_o):
    bsz, seqlen, _ = u.shape
    proj = u @ w_in
    split_at = [int(v) for v in np.cumsum(proj_sizes())[:-1]]
    gl, cb, cc, cx, z, xbc, dt = jnp.split(proj, split_at, axis=-1)

    y_conv = cb * causal_depthwise_conv(cc * cx, conv_w)
    p_conv = y_conv @ w_conv_out

    xbc = jax.nn.silu(causal_depthwise_conv(xbc, ssm_conv_w) + ssm_conv_b.astype(xbc.dtype))
    xbc = xbc.astype(jnp.float32)
    xs, bs, cs = jnp.split(xbc, [D_SSM, D_SSM + SSM_GROUPS * SSM_STATE], axis=-1)
    xs = xs.reshape(bsz, seqlen, SSM_HEADS, SSM_HEAD_DIM)
    bs = bs.reshape(bsz, seqlen, SSM_GROUPS, SSM_STATE)
    cs = cs.reshape(bsz, seqlen, SSM_GROUPS, SSM_STATE)
    dt = jax.nn.softplus(dt.astype(jnp.float32) + dt_bias.astype(jnp.float32))
    a = -jnp.exp(a_log.astype(jnp.float32))
    y = ssd_scan(xs * dt[..., None], dt * a, bs, cs)
    y = y + d_skip.astype(jnp.float32)[:, None] * xs
    y = y.reshape(bsz, seqlen, D_SSM) * jax.nn.silu(z.astype(jnp.float32))
    yg = y.reshape(bsz, seqlen, SSM_GROUPS, D_SSM // SSM_GROUPS)
    yg = yg * lax.rsqrt(jnp.mean(yg * yg, axis=-1, keepdims=True) + EPS)
    y = (yg.reshape(bsz, seqlen, D_SSM) * ssm_norm_w.astype(jnp.float32)).astype(u.dtype)
    p_ssm = y @ w_ssm_out

    g_conv, g_ssm = jnp.split(jax.nn.sigmoid(gl), 2, axis=-1)
    merged = g_conv * p_conv + g_ssm * p_ssm
    return merged @ w_o

def first_inputs(seed: int = 0) -> dict:
    key = jax.random.key(seed)
    ks = jax.random.split(key, 24)
    d_proj = sum(proj_sizes())
    f32 = jnp.float32

    def nrm(k, shape, scale):
        return jax.random.normal(k, shape, f32) * scale

    dt0 = jnp.exp(jax.random.uniform(ks[10], (DEPTH, SSM_HEADS), f32,
                                     np.log(DT_MIN), np.log(DT_MAX)))
    dt_bias = dt0 + jnp.log(-jnp.expm1(-dt0))
    return {
        "x": nrm(ks[0], (BATCH, SEQ, D_MODEL), 1.0),
        "c": nrm(ks[1], (BATCH, D_MODEL), 1.0),
        "w_ada": nrm(ks[2], (DEPTH, D_MODEL, N_MOD * D_MODEL), 0.5 * D_MODEL ** -0.5),
        "b_ada": nrm(ks[3], (DEPTH, N_MOD * D_MODEL), 0.02),
        "ln1": 1.0 + nrm(ks[4], (DEPTH, D_MODEL), 0.1),
        "ln2": 1.0 + nrm(ks[5], (DEPTH, D_MODEL), 0.1),
        "w_in": nrm(ks[6], (DEPTH, D_MODEL, d_proj), D_MODEL ** -0.5),
        "conv_w": nrm(ks[7], (DEPTH, CONV_WIDTH, CONV_DIM), CONV_WIDTH ** -0.5),
        "ssm_conv_w": nrm(ks[8], (DEPTH, SSM_CONV_WIDTH, SSM_CONV_DIM), SSM_CONV_WIDTH ** -0.5),
        "ssm_conv_b": nrm(ks[9], (DEPTH, SSM_CONV_DIM), 0.01),
        "dt_bias": dt_bias,
        "a_log": jnp.log(jax.random.uniform(ks[11], (DEPTH, SSM_HEADS), f32, 1.0, 16.0)),
        "d_skip": 1.0 + nrm(ks[12], (DEPTH, SSM_HEADS), 0.1),
        "ssm_norm_w": 1.0 + nrm(ks[13], (DEPTH, D_SSM), 0.1),
        "w_conv_out": nrm(ks[14], (DEPTH, CONV_DIM, D_MODEL), CONV_DIM ** -0.5),
        "w_ssm_out": nrm(ks[15], (DEPTH, D_SSM, D_MODEL), D_SSM ** -0.5),
        "w_o": nrm(ks[16], (DEPTH, D_MODEL, D_MODEL), D_MODEL ** -0.5),
        "w_up": nrm(ks[17], (DEPTH, D_MODEL, D_FF), D_MODEL ** -0.5),
        "w_down": nrm(ks[18], (DEPTH, D_FF, D_MODEL), D_FF ** -0.5),
        "final_norm": 1.0 + nrm(ks[19], (D_MODEL,), 0.1),
    }

def first_block(x, c, w_ada, b_ada, ln1, ln2, w_in, conv_w, ssm_conv_w, ssm_conv_b,
              dt_bias, a_log, d_skip, ssm_norm_w, w_conv_out, w_ssm_out, w_o,
              w_up, w_down, final_norm):
    bsz = x.shape[0]
    c_act = jax.nn.silu(c)
    for i in range(DEPTH):
        mod = (c_act @ w_ada[i] + b_ada[i]).reshape(bsz, N_MOD, D_MODEL)[:, :, None, :]
        shift1, scale1, gate1 = mod[:, 0], mod[:, 1], mod[:, 2]
        shift2, scale2, gate2 = mod[:, 3], mod[:, 4], mod[:, 5]

        u = rms_norm(x, ln1[i]) * (1.0 + scale1) + shift1
        mix = mixer_sublayer(u, w_in[i], conv_w[i], ssm_conv_w[i], ssm_conv_b[i], dt_bias[i],
                             a_log[i], d_skip[i], ssm_norm_w[i], w_conv_out[i],
                             w_ssm_out[i], w_o[i])
        x = x + gate1 * mix

        u2 = rms_norm(x, ln2[i]) * (1.0 + scale2) + shift2
        hid = jnp.square(jax.nn.relu(u2 @ w_up[i]))
        x = x + gate2 * (hid @ w_down[i])
    return rms_norm(x, final_norm)


HEAD_DIM = 64
FOX_HEADS = 8
DIFF_HEADS = 4
FOX_WIDTH = FOX_HEADS * HEAD_DIM
DIFF_WIDTH = DIFF_HEADS * 2 * HEAD_DIM
MIX_WIDTH = FOX_WIDTH + DIFF_WIDTH
IN_WIDTH = 3 * FOX_WIDTH + FOX_HEADS + 3 * DIFF_WIDTH
D_FF_2 = ((8 * D_MODEL // 3 + 255) // 256) * 256
BLOCK_Q = 128


def _rms(x, g):
    xf = x.astype(jnp.float32)
    y = xf * lax.rsqrt(jnp.mean(xf * xf, axis=-1, keepdims=True) + EPS)
    return (y * g.astype(jnp.float32)).astype(x.dtype)

def _to_blocks(t):
    b, h, s = t.shape[:3]
    nb = s // BLOCK_Q
    t = t.reshape((b, h, nb, BLOCK_Q) + t.shape[3:])
    return jnp.moveaxis(t, 2, 0)

def _from_blocks(t):
    nb, b, h, bq, d = t.shape
    return jnp.moveaxis(t, 0, 2).reshape(b, h, nb * bq, d)

def _fox_attention(q, k, v, log_f):
    s_len = q.shape[2]
    scale = 1.0 / math.sqrt(q.shape[-1])
    cum = jnp.cumsum(log_f, axis=-1)
    key_pos = jnp.arange(s_len)
    starts = jnp.arange(s_len // BLOCK_Q) * BLOCK_Q

    def one_block(args):
        qi, ci, st = args
        s = jnp.einsum('bhqd,bhkd->bhqk', qi, k, preferred_element_type=jnp.float32) * scale
        s = s + ci[..., :, None] - cum[..., None, :]
        qpos = st + jnp.arange(BLOCK_Q)
        mask = key_pos[None, :] <= qpos[:, None]
        p = jax.nn.softmax(jnp.where(mask, s, -jnp.inf), axis=-1)
        return jnp.einsum('bhqk,bhkd->bhqd', p.astype(v.dtype), v)

    out = lax.map(one_block, (_to_blocks(q), _to_blocks(cum), starts))
    return _from_blocks(out)

def _diff_attention(q1, q2, k1, k2, v, lam, slopes):
    s_len = q1.shape[2]
    scale = 1.0 / math.sqrt(q1.shape[-1])
    key_pos = jnp.arange(s_len)
    starts = jnp.arange(s_len // BLOCK_Q) * BLOCK_Q

    def one_block(args):
        q1i, q2i, st = args
        qpos = st + jnp.arange(BLOCK_Q)
        dist = (qpos[:, None] - key_pos[None, :]).astype(jnp.float32)
        alibi = -slopes[:, None, None] * dist
        mask = dist >= 0
        s1 = jnp.einsum('bhqd,bhkd->bhqk', q1i, k1, preferred_element_type=jnp.float32) * scale + alibi
        s2 = jnp.einsum('bhqd,bhkd->bhqk', q2i, k2, preferred_element_type=jnp.float32) * scale + alibi
        p = (jax.nn.softmax(jnp.where(mask, s1, -jnp.inf), axis=-1)
             - lam * jax.nn.softmax(jnp.where(mask, s2, -jnp.inf), axis=-1))
        return jnp.einsum('bhqk,bhkd->bhqd', p.astype(v.dtype), v)

    out = lax.map(one_block, (_to_blocks(q1), _to_blocks(q2), starts))
    return _from_blocks(out)

def _modulate(x, g, shift, scale):
    return _rms(x, g) * (1.0 + scale[:, None, :]) + shift[:, None, :]

def second_inputs(seed: int = 0) -> dict:
    key = jax.random.key(seed)
    ks = jax.random.split(key, 20)
    f32 = jnp.float32
    nrm = lambda k, shape, s: jax.random.normal(k, shape, f32) * s
    d = D_MODEL
    return {
        "x": nrm(ks[0], (BATCH, SEQ, d), 1.0),
        "c": nrm(ks[1], (BATCH, d), 1.0),
        "ln1_g": 1.0 + nrm(ks[2], (DEPTH, d), 0.02),
        "ln2_g": 1.0 + nrm(ks[3], (DEPTH, d), 0.02),
        "w_ada": nrm(ks[4], (DEPTH, d, 6 * d), 0.5 * d ** -0.5),
        "b_ada": nrm(ks[5], (DEPTH, 6 * d), 0.02),
        "w_in": nrm(ks[6], (DEPTH, d, IN_WIDTH), d ** -0.5),
        "b_f": 1.5 + nrm(ks[7], (DEPTH, FOX_HEADS), 0.1),
        "fox_qk_g": 1.0 + nrm(ks[8], (DEPTH, 2, HEAD_DIM), 0.02),
        "diff_qk_g": 1.0 + nrm(ks[9], (DEPTH, 2, HEAD_DIM), 0.02),
        "diff_lam": nrm(ks[10], (DEPTH, 4, HEAD_DIM), 0.1),
        "diff_norm_g": 1.0 + nrm(ks[11], (DEPTH, 2 * HEAD_DIM), 0.02),
        "w_out": nrm(ks[12], (DEPTH, MIX_WIDTH, d), MIX_WIDTH ** -0.5),
        "w_gate": nrm(ks[13], (DEPTH, d, D_FF_2), d ** -0.5),
        "w_up": nrm(ks[14], (DEPTH, d, D_FF_2), d ** -0.5),
        "w_down": nrm(ks[15], (DEPTH, D_FF_2, d), D_FF_2 ** -0.5),
    }

def second_block(x, c, ln1_g, ln2_g, w_ada, b_ada, w_in, b_f, fox_qk_g, diff_qk_g,
              diff_lam, diff_norm_g, w_out, w_gate, w_up, w_down):
    b, s, d = x.shape
    cond = jax.nn.silu(c)
    slopes = 2.0 ** (-8.0 * jnp.arange(1, DIFF_HEADS + 1, dtype=jnp.float32) / DIFF_HEADS)
    splits = np.cumsum([FOX_WIDTH, FOX_WIDTH, FOX_WIDTH, FOX_HEADS,
                        DIFF_WIDTH, DIFF_WIDTH]).tolist()

    for l in range(DEPTH):
        mod = cond @ w_ada[l] + b_ada[l]
        sh1, sc1, g1, sh2, sc2, g2 = jnp.split(mod, 6, axis=-1)

        h = _modulate(x, ln1_g[l], sh1, sc1)
        u = h @ w_in[l]
        fq, fk, fv, fg, dq, dk, dv = jnp.split(u, splits, axis=-1)

        heads = lambda t, n, hd: t.reshape(b, s, n, hd).transpose(0, 2, 1, 3)
        fq = _rms(heads(fq, FOX_HEADS, HEAD_DIM), fox_qk_g[l, 0])
        fk = _rms(heads(fk, FOX_HEADS, HEAD_DIM), fox_qk_g[l, 1])
        fv = heads(fv, FOX_HEADS, HEAD_DIM)
        log_f = jax.nn.log_sigmoid(fg.astype(jnp.float32) + b_f[l].astype(jnp.float32))
        log_f = log_f.transpose(0, 2, 1)
        fox_out = _fox_attention(fq, fk, fv, log_f)

        dq = dq.reshape(b, s, DIFF_HEADS, 2, HEAD_DIM).transpose(0, 2, 3, 1, 4)
        dk = dk.reshape(b, s, DIFF_HEADS, 2, HEAD_DIM).transpose(0, 2, 3, 1, 4)
        dq = _rms(dq, diff_qk_g[l, 0])
        dk = _rms(dk, diff_qk_g[l, 1])
        dv = heads(dv, DIFF_HEADS, 2 * HEAD_DIM)
        lam_init = 0.8 - 0.6 * math.exp(-0.3 * l)
        lv = diff_lam[l].astype(jnp.float32)
        lam = jnp.exp(jnp.sum(lv[0] * lv[1])) - jnp.exp(jnp.sum(lv[2] * lv[3])) + lam_init
        diff_out = _diff_attention(dq[:, :, 0], dq[:, :, 1], dk[:, :, 0], dk[:, :, 1], dv, lam, slopes)
        diff_out = _rms(diff_out, diff_norm_g[l]) * (1.0 - lam_init)

        mixed = jnp.concatenate([
            fox_out.transpose(0, 2, 1, 3).reshape(b, s, FOX_WIDTH),
            diff_out.transpose(0, 2, 1, 3).reshape(b, s, DIFF_WIDTH)], axis=-1)
        x = x + g1[:, None, :] * (mixed @ w_out[l])

        h2 = _modulate(x, ln2_g[l], sh2, sc2)
        y = (jax.nn.silu(h2 @ w_gate[l]) * (h2 @ w_up[l])) @ w_down[l]
        x = x + g2[:, None, :] * y
    return x


def setup_inputs(seed=0):
    out = dict(first_inputs(seed))
    for name, value in second_inputs(seed + 1).items():
        if name != "x":
            out[name + "_2"] = value
    return out


def reference(
    x, c, w_ada, b_ada, ln1, ln2, w_in, conv_w, ssm_conv_w, ssm_conv_b, dt_bias, a_log, d_skip,
    ssm_norm_w, w_conv_out, w_ssm_out, w_o, w_up, w_down, final_norm, c_2, ln1_g_2, ln2_g_2,
    w_ada_2, b_ada_2, w_in_2, b_f_2, fox_qk_g_2, diff_qk_g_2, diff_lam_2, diff_norm_g_2,
    w_out_2, w_gate_2, w_up_2, w_down_2,
):
    x = first_block(
        x, c, w_ada, b_ada, ln1, ln2, w_in, conv_w, ssm_conv_w, ssm_conv_b, dt_bias, a_log,
        d_skip, ssm_norm_w, w_conv_out, w_ssm_out, w_o, w_up, w_down, final_norm,
    )
    return second_block(
        x, c_2, ln1_g_2, ln2_g_2, w_ada_2, b_ada_2, w_in_2, b_f_2, fox_qk_g_2, diff_qk_g_2,
        diff_lam_2, diff_norm_g_2, w_out_2, w_gate_2, w_up_2, w_down_2,
    )


_drawn_inputs = setup_inputs


def setup_inputs(seed=0):
    import zlib

    import numpy as np

    out = dict(_drawn_inputs(seed))
    spreads = {}
    factors = {'ssm_conv_b': 8.0,
     'd_skip': 7.037,
     'ssm_norm_w': 3.275,
     'ln1_g_2': 8.0,
     'ln2_g_2': 8.0,
     'b_f_2': 8.0,
     'fox_qk_g_2': 8.0,
     'diff_qk_g_2': 8.0,
     'diff_lam_2': 3.197,
     'diff_norm_g_2': 26.428}
    for name, (base, spread) in spreads.items():
        noise = np.random.default_rng([zlib.crc32(name.encode()), seed]).standard_normal(out[name].shape)
        drawn = base * np.exp(spread * noise) if base else spread * noise
        out[name] = __import__('jax').numpy.asarray(drawn.astype(out[name].dtype))
    for name, factor in factors.items():
        out[name] = (out[name] * factor).astype(out[name].dtype)
    return out
```

```python
from contextlib import ExitStack

import numpy as np
import concourse.bass as bass
from concourse import mybir

F32 = mybir.dt.float32
F32R = mybir.dt.float32r
I32 = mybir.dt.int32
ALU = mybir.AluOpType
ACT = mybir.ActivationFunctionType
AX_X = mybir.AxisListType.X

P = 128
T = 256
TT = T // P
D = 1024
KB = D // P
CW = 256
NB = CW // P
DSSM = 2 * D
HEADS = 32
GROUPS = 8
HD = 64
DFF1 = 4 * D
DFF2 = 2816
EPS = 1e-6
NEG = -1.0e30
LAM_INIT = 0.2
NRAW, NHL, NACC, NF = 3, 3, 3, 4

U1, YC, YS, MG, U2, HID, U3, MX, U4, HID2 = 0, 8, 16, 32, 40, 48, 80, 88, 96, 104


class Step:

    def __init__(self, kind, j, src, kts, cols, act, kt0=0, k=0, nk=1):
        self.kind, self.j, self.src, self.kts, self.cols = kind, j, src, kts, cols
        self.act, self.kt0, self.k, self.nk = act, kt0, k, nk
        self.tokens_out = kind in ("dt", "fv", "dv", "fg")
        self.last = k == nk - 1
        self.g = None


def plan(a):
    steps = []

    def add(kind, j, w, r0, rows, c0, cols, act, kt0=0, k=0, nk=1):
        steps.append(Step(kind, j, w[r0:r0 + rows, c0:c0 + cols], rows // P, cols, act, kt0, k, nk))

    w_in = a["w_in"][0]
    GL, CB, CC, CX, Z, XBC = 0, 2 * D, 3 * D, 4 * D, 5 * D, 5 * D + DSSM
    DT = XBC + DSSM + 2 * GROUPS * P
    add("dt", 0, w_in, 0, D, DT, HEADS, U1)
    for j in range(16):
        add("xbc", j, w_in, 0, D, XBC + (2 * j + 16) % 32 * P, CW, U1)
    for j in range(4):
        add("cc", j, w_in, 0, D, CC + j * CW, CW, U1)
        add("cx", j, w_in, 0, D, CX + j * CW, CW, U1)
        add("cb", j, w_in, 0, D, CB + j * CW, CW, U1)
    for j in range(4):
        add("gc", j, w_in, 0, D, GL + j * CW, CW, U1)
        add("co", j, a["w_conv_out"][0], 0, D, j * CW, CW, YC)
    for j in range(8):
        add("z", j, w_in, 0, D, Z + j * CW, CW, U1)
    for j in range(4):
        add("gs", j, w_in, 0, D, GL + D + j * CW, CW, U1)
        for k in range(2):
            add("so", j, a["w_ssm_out"][0], k * D, D, j * CW, CW, YS, k * KB, k, 2)
    for j in range(4):
        add("wo", j, a["w_o"][0], 0, D, j * CW, CW, MG)
    for j in range(DFF1 // CW):
        add("up", j, a["w_up"][0], 0, D, j * CW, CW, U2)
    for j in range(4):
        for k in range(4):
            add("dn", j, a["w_down"][0], k * D, D, j * CW, CW, HID, k * KB, k, 4)
    w2 = a["w_in_2"][0]
    for kind, j, c0 in (("dq", 0, 1544), ("dq", 1, 1800), ("dk", 0, 2056), ("dk", 1, 2312),
                        ("dv", 0, 2568), ("dv", 1, 2824), ("fg", 0, 1536), ("fq", 0, 0), ("fk", 0, 512),
                        ("fq", 1, 256), ("fk", 1, 768), ("fv", 0, 1024), ("fv", 1, 1280)):
        add(kind, j, w2, 0, D, c0, 8 if kind == "fg" else CW, U3)
    for j in range(4):
        add("o2", j, a["w_out_2"][0], 0, D, j * CW, CW, MX)
    for j in range(DFF2 // CW):
        add("gt", j, a["w_gate_2"][0], 0, D, j * CW, CW, U4)
        add("u2", j, a["w_up_2"][0], 0, D, j * CW, CW, U4)
    for j in range(4):
        for k, rows in enumerate((D, D, DFF2 - 2 * D)):
            add("d2", j, a["w_down_2"][0], k * D, rows, j * CW, CW, HID2, k * KB, k, 3)
    g = 0
    for s in steps:
        if s.k == 0:
            s.g = g
            g += NB
        else:
            s.g = prev.g
        prev = s
    return steps


def build(nc, a, out):
    steps = plan(a)
    NS = len(steps)
    first = {}
    for n, s in enumerate(steps):
        first.setdefault((s.kind, s.j, s.k), n)
    start_of = {}
    for n, s in enumerate(steps):
        start_of.setdefault(s.kind, n)
    QK_ORDER = [(s.kind, s.j) for s in steps if s.kind in ("dq", "dk", "fq", "fk")]
    X0, C0, Z0, I0 = (start_of[k] for k in ("xbc", "cc", "z", "dq"))
    SCAN0 = C0 + 1
    NA0 = 2 * D // CW
    NCOL = 12 * KB - NB * NA0
    XCOL = 2 * KB
    col_step = [1 + m if m < XCOL else SCAN0 + 17 + m - XCOL for m in range(NCOL)]
    col_at = {n: m for m, n in enumerate(col_step)}
    MOD1_AT, MOD2_AT, MOD3_AT = (col_step[c - NB * NA0 - 1] + 3 for c in (48, 64, 96))

    stream = [("step", 0), ("step", 1)] + [("ada", n) for n in range(NA0)]
    for n in range(2, NS):
        stream.append(("step", n))
        if n - 4 in col_at:
            stream.append(("col", col_at[n - 4]))
    raw_stream = [item for item in stream if item[0] != "col"]
    raw_at = {item: r for r, item in enumerate(raw_stream)}

    with ExitStack() as ctx, ExitStack() as programs:
        def sb(name, shape, dt=F32, stack=ctx):
            return stack.enter_context(nc.sbuf_tensor(name, shape, dt))

        sems = {}

        class Sems:
            def __call__(self, name):
                if name not in sems:
                    sems[name] = ctx.enter_context(nc.semaphore(name))
                return sems[name]

        S = Sems()

        raw = sb("raw", [P, NRAW, KB, CW])
        w_hi = sb("w_hi", [P, NHL, KB, CW], F32R)
        w_lo = sb("w_lo", [P, NHL, KB, CW], F32R)
        xT = sb("xT", [P, KB, T])
        uh = sb("uh", [P, KB, T], F32R)
        ul = sb("ul", [P, KB, T], F32R)
        par = sb("par", [P, 3, P])
        cact = sb("cact", [P, 16])
        mod = sb("mod", [P, 96])
        gain = sb("gain", [P, 5, KB])
        small = sb("small", [P, 16])
        ident = sb("ident", [P, P])
        ones = sb("ones", [P, P])
        blk64 = sb("blk64", [P, P])
        tri = sb("tri", [P, T])
        min_st = sb("min_st", [P, T])
        mask_ts = sb("mask_ts", [P, 3 * P])
        dist_ts = sb("dist_ts", [P, 3 * P])
        eps = sb("eps", [P, 1])
        fr = sb("fr", [P, NF, T])
        stg = sb("stg", [P, 2, T + 3])
        cv = sb("cv", [P, 2, T])
        cct = sb("cct", [P, 2, T])
        gt = sb("gt", [P, 2, T])
        sq = sb("sq", [P, 4, T])
        rt = sb("rt", [P, 2, T])
        rb = sb("rb", [P, 2, T])
        maps = sb("maps", [P, 3 * 2 * 3 * P])
        seg, ex, sc = (maps[:, i * 6 * P:(i + 1) * 6 * P].rearrange("p (a b) -> p a b", b=3 * P) for i in range(3))
        colw = maps[:, 0:2 * KB * P].rearrange("p (s k c) -> p s k c", s=2, c=P)
        cols = maps[:, 2 * KB * P:(2 * KB + 2) * P].rearrange("p (s c) -> p s c", c=P)
        nmx = sb("nmx", [P, 2, 2])
        rs = sb("rs", [P, 2, 2])
        rr = sb("rr", [P, 2, 2])
        dtr = cct[:, :, :].rearrange("p a b -> p (a b)")[:, 0:6 * TT * HEADS]\
            .rearrange("p (a b) -> p a b", b=TT * HEADS)
        dt_sb = sb("dt_sb", [P, TT, HEADS])
        dta = sb("dta", [P, TT, HEADS])
        nac = sb("nac", [P, TT, HEADS])
        hb = sb("hb", [P, 3, HEADS])
        nega = sb("nega", [P, HEADS])
        dsk = sb("dsk", [P, HEADS // 2])
        bf = sb("bf", [P, 8])
        lamw = gt[:, 0, :].rearrange("p (a b) -> p a b", b=HD)
        lf = sb("lf", [P, TT, 8])
        fcum = sb("fcum", [P, TT, 8])

        arena = ExitStack()
        xs = sb("xs", [P, 16, T], F32, arena)
        bct = sb("bct", [P, 16, T], F32, arena)
        xdt = sb("xdt", [P, TT, DSSM], F32, arena)
        ych = sb("ych", [P, KB, T], F32R, arena)
        ycl = sb("ycl", [P, KB, T], F32R, arena)
        mc = sb("mc", [P, KB, T], F32, arena)
        arena.close()
        arena = ExitStack()
        sb("skip_xs", [P, 16, T], F32, arena)
        ysh = sb("ysh", [P, 16, T], F32R, arena)
        ysl = sb("ysl", [P, 16, T], F32R, arena)
        arena.close()
        arena = ExitStack()
        hidh = sb("hidh", [P, 32, T], F32R, arena)
        hidl = sb("hidl", [P, 32, T], F32R, arena)
        outb = sb("outb", [P, TT, D], F32, arena)
        arena.close()
        arena = ExitStack()
        qk = sb("qk", [P, 16, T], F32, arena)
        v = sb("v", [P, TT, D], F32, arena)
        mxh = sb("mxh", [P, KB, T], F32R, arena)
        mxl = sb("mxl", [P, KB, T], F32R, arena)
        arena.close()
        sb("arena", [P, 18, D])

        acc = [ctx.enter_context(nc.psum_tensor(f"acc{i}", [P, 512], F32)) for i in range(NACC)]
        M0, M1, M2, M3, M4 = (ctx.enter_context(nc.psum_tensor(f"m{i}", [P, 512], F32)) for i in range(5))

        c_cols, ln_cols, ada_b = par[:, 0, 0:16], par[:, 0, 16:32], par[:, 0, 32:128]
        conv_w, norm_w, final_w = par[:, 1, 0:24], par[:, 1, 24:40], par[:, 1, 40:48]
        ln2_cols, ssm_b, qk_gain, dn_gain = par[:, 1, 48:64], par[:, 1, 64:96], par[:, 1, 96:100], par[:, 1, 100:101]
        ssm_w = par[:, 2, :]
        SH = [mod[:, 0:8], mod[:, 24:32], None, mod[:, 48:56], mod[:, 72:80]]
        SCL = [mod[:, 8:16], mod[:, 32:40], None, mod[:, 56:64], mod[:, 80:88]]
        GATE = [mod[:, 16:24], mod[:, 40:48], mod[:, 64:72], mod[:, 88:96]]
        LN = [ln_cols[:, 0:8], ln_cols[:, 8:16], None, ln2_cols[:, 0:8], ln2_cols[:, 8:16]]
        NORM_U = [U1, U2, None, U3, U4]
        NEG_LAM = small[:, 0:1]

        def mod_bank(col):
            return M0 if col < NB * NA0 + XCOL else M1 if col < 48 else M2 if col < 64 else M3

        def dest(i):
            for base, hi, lo, n0 in ((HID2, hidh, hidl, 0), (U4, uh, ul, 0), (MX, mxh, mxl, None), (U3, uh, ul, 0),
                                     (HID, hidh, hidl, 0), (U2, uh, ul, 0), (MG, ych, ycl, 0), (YS, ysh, ysl, 0),
                                     (YC, ych, ycl, 0), (U1, uh, ul, 0)):
                if i >= base:
                    b = i - base
                    if n0 is None:
                        b = (b + 4) % 8
                    return hi[:, b, :], lo[:, b, :]

        def operands(base):
            return {U1: (uh, ul), YC: (ych, ycl), YS: (ysh, ysl), MG: (ych, ycl), U2: (uh, ul), HID: (hidh, hidl),
                    U3: (uh, ul), MX: (mxh, mxl), U4: (uh, ul), HID2: (hidh, hidl)}[base]

        def raw_of(item, s=None):
            slot = raw_at[item] % NRAW
            return raw[:, slot, 0:s.kts, 0:s.cols] if s else raw[:, slot, :, :]

        def wait_raw(eng, item):
            r = raw_at[item]
            eng.wait_ge(S(f"raw_in{r % NRAW}"), 16 * (r // NRAW + 1))

        rows = seg[:, :, :].rearrange("p a (b c) -> p (a b) c", c=P)
        N_PAR, N_VEC = 18, 5
        N_CONST = 20

        def drained(s, nb):
            i = NB * s.j + nb
            if s.kind in ("dq", "dk", "fq", "fk"):
                return "qk_raw", NB * QK_ORDER.index((s.kind, s.j)) + nb + 1
            return {
                "dt": ("dt_z", nb + 1), "fg": ("fg_z", nb + 1), "xbc": ("cv_init", i + 1), "cc": ("cc_out", i + 1),
                "cx": ("cx_in", i + 1), "cb": ("f_ready", YC + i + 1), "gc": ("gate", i + 1), "gs": ("gate", 9 + i),
                "co": ("gate_used", i + 1), "so": ("gate_used", 9 + i), "z": ("sz_done", i + 1),
                "wo": ("x_ready", KB + i + 1), "dn": ("x_ready", 2 * KB + i + 1), "o2": ("x_ready", 4 * KB + i + 1),
                "d2": ("x_ready", 5 * KB + i + 1), "up": ("relu", i + 1), "gt": ("silu_g", i + 1),
                "u2": ("f_ready", HID2 + i + 1), "dv": ("v_out", i + 1), "fv": ("v_out", 5 + i),
            }[s.kind]

        def product_of(w):
            if not 0 <= w < 16 or (w < 8 and w % 2 == 0):
                return None
            return w // 2 if w < 8 else w - 4

        unfinished = [0]
        for s_ in steps:
            unfinished.append(unfinished[-1] + (not s_.last))

        def wait_step(eng, n):
            if steps[n].last:
                eng.wait_ge(S("acc_ready"), steps[n].g + NB)
            else:
                eng.wait_ge(S("part_done"), unfinished[n + 1])

        def row_loads():
            st = rows
            def vec(name, n):
                ap = a[name]
                return ap[0].rearrange("(b f) -> b f", f=P) if len(ap.shape) == 2 else ap.rearrange("(b f) -> b f", f=P)
            return [
                (st[0:8, 0, :], vec("c", 8)), (st[8:16, 0, :], vec("c_2", 8)),
                (st[16:24, 0, :], vec("ln1", 8)), (st[24:32, 0, :], vec("ln2", 8)),
                (st[32:80, 0, :], vec("b_ada", 48)), (st[80:128, 0, :], vec("b_ada_2", 48)),
                (st[0:24, 1, :], a["conv_w"][0].rearrange("k (b f) -> (k b) f", f=P)),
                (st[24:40, 1, :], vec("ssm_norm_w", 16)), (st[40:48, 1, :], vec("final_norm", 8)),
                (st[48:56, 1, :], vec("ln1_g_2", 8)), (st[56:64, 1, :], vec("ln2_g_2", 8)),
                (st[64:96, 1, :], vec("ssm_conv_b", 32)),
                (st[96:98, 1, 0:HD], a["fox_qk_g_2"][0]), (st[96:98, 1, HD:P], a["fox_qk_g_2"][0]),
                (st[98:100, 1, 0:HD], a["diff_qk_g_2"][0]), (st[98:100, 1, HD:P], a["diff_qk_g_2"][0]),
                (st[100:101, 1, :], a["diff_norm_g_2"]),
                (st[:, 2, :], a["ssm_conv_w"][0].rearrange("k (b f) -> (k b) f", f=P)),
            ]

        def row_vectors():
            return [(hb[:, 0, :], a["dt_bias"].to_broadcast([P, HEADS])), (hb[:, 1, :], a["a_log"].to_broadcast([P, HEADS])),
                    (hb[:, 2, :], a["d_skip"].to_broadcast([P, HEADS])), (bf[:, :], a["b_f_2"].to_broadcast([P, 8])),
                    (lamw[:, :, :].rearrange("p a b -> p (a b)"),
                     a["diff_lam_2"].rearrange("o a b -> o (a b)").to_broadcast([P, 4 * HD]))]

        block = programs.enter_context(nc.Block())

        @block.sync
        def _(sp):
            x_tok = xdt[:, :, 0:D]
            sp.dma_start(x_tok, a["x"][0].rearrange("(a p) d -> p a d", p=P)).then_inc(S("x_in"), 16)
            sp.wait_ge(S("par_zero"), 1)
            for dst, src in row_loads():
                sp.dma_start(dst, src).then_inc(S("par_in"), 16)
            for item in stream:
                kind, n = item
                if kind == "col":
                    if n == 0:
                        sp.wait_ge(S("par_done"), 1)
                    elif n == XCOL:
                        sp.wait_ge(S("y_done"), HEADS)
                    if n >= 2:
                        sp.wait_ge(S("col_sum"), n - 1)
                    w, c = (a["w_ada"][0], n + NB * NA0) if n + NB * NA0 < 48 else (a["w_ada_2"][0], n + NB * NA0 - 48)
                    sp.dma_start(colw[:, n % 2, :, :], w[:, c * P:(c + 1) * P].rearrange("(k p) n -> p k n", p=P))\
                      .then_inc(S(f"col_in{n % 2}"), 16)
                    continue
                r = raw_at[item]
                if r == 1:
                    for dst, src in row_vectors():
                        sp.dma_start(dst, src).then_inc(S("vec_in"), 16)
                if r >= NRAW:
                    before, b = raw_stream[r - NRAW]
                    if before == "step":
                        sp.wait_ge(S("lo_ready"), b + 1)
                    else:
                        sp.wait_ge(S("ada_used"), b + 1)
                if kind == "step":
                    s = steps[n]
                    dst, src = raw_of(item, s), s.src
                else:
                    dst, src = raw_of(item), a["w_ada"][0][:, n * CW:(n + 1) * CW]
                sp.dma_start(dst, src.rearrange("(k p) n -> p k n", p=P)).then_inc(S(f"raw_in{r % NRAW}"), 16)
            for b in range(KB):
                sp.wait_ge(S("out_ready"), b + 1)
                sp.dma_start(out[0].rearrange("(a p) d -> p a d", p=P)[:, :, b * P:(b + 1) * P],
                             outb[:, :, b * P:(b + 1) * P]).then_inc(S("out_done"), 16)
            sp.wait_ge(S("out_done"), 16 * KB)

        @block.gpsimd
        def _(pool):
            pool.memset(rows[:, 0:3, :], 0.0).then_inc(S("par_zero"), 1)
            pool.memset(ident[:, :], 0.0).then_inc(S("pc"), 1)
            pool.memset(ones[:, :], 1.0).then_inc(S("pc"), 1)
            pool.memset(blk64[:, :], 0.0).then_inc(S("pc"), 1)
            pool.memset(tri[:, :], 1.0).then_inc(S("pc"), 1)
            pool.memset(min_st[:, :], 0.0).then_inc(S("pc"), 1)
            pool.memset(mask_ts[:, :], 0.0).then_inc(S("pc"), 1)
            pool.memset(eps[:, :], EPS).then_inc(S("pc"), 1)
            pool.memset(stg[:, :, 0:3], 0.0).then_inc(S("pc"), 1)
            distf = ex[:, 0, :]
            disti = ex[:, 1, :].bitcast(I32)
            pool.iota(disti[:, 0:P], pattern=[[1, P]], base=0, channel_multiplier=-1).then_inc(S("pc"), 1)
            pool.iota(disti[:, P:3 * P], pattern=[[1, T]], base=-P, channel_multiplier=-1).then_inc(S("pc"), 1)
            pool.wait_ge(S("pc"), 10)
            pool.affine_select(out=ident[:, :], in_=ident[:, :], compare_op=ALU.not_equal, fill=1.0, base=0,
                               pattern=[[-1, P]], channel_multiplier=1).then_inc(S("pc"), 1)
            for i, o in enumerate((0, HD)):
                pool.wait_ge(S("pc"), 11 + i)
                pool.memset(blk64[o:o + HD, o:o + HD], 1.0).then_inc(S("pc"), 1)
            pool.wait_ge(S("pc"), 13)
            pool.affine_select(out=tri[:, :], in_=tri[:, :], compare_op=ALU.is_ge, fill=0.0, base=0,
                               pattern=[[1, T]], channel_multiplier=-1).then_inc(S("pc"), 1)
            pool.affine_select(out=min_st[:, :], in_=min_st[:, :], compare_op=ALU.is_ge, fill=NEG, base=0,
                               pattern=[[1, T]], channel_multiplier=-1).then_inc(S("pc"), 1)
            pool.tensor_copy(distf, disti).then_inc(S("pc"), 1)
            pool.wait_ge(S("pc"), 16)
            for dst, src in ((mask_ts, mask_ts[:, :]), (dist_ts, distf)):
                pool.affine_select(out=dst[:, 0:P], in_=src[:, 0:P], compare_op=ALU.is_ge, fill=NEG, base=0,
                                   pattern=[[-1, P]], channel_multiplier=1).then_inc(S("pc"), 1)
                pool.affine_select(out=dst[:, P:3 * P], in_=src[:, P:3 * P], compare_op=ALU.is_ge, fill=NEG, base=P,
                                   pattern=[[-1, T]], channel_multiplier=1).then_inc(S("pc"), 1)

            def lo_part(i):
                hi, lo = dest(i)
                pool.wait_ge(S("act_hi"), i + 1)
                pool.tensor_tensor(lo, fr[:, i % NF, :], hi.bitcast(F32), ALU.subtract).then_inc(S("act_lo"), 1)

            for i in range(U1, YC):
                lo_part(i)
            for n in range(NS):
                s = steps[n]
                for nb in range(NB):
                    if s.kind == "cb":
                        lo_part(YC + NB * s.j + nb)
                    q = NB * (n - SCAN0) + nb
                    if 0 <= q < HEADS:
                        pool.wait_ge(S("exp_done"), q + 1)
                        pool.wait_ge(S("sc_done"), q // 4 + 1)
                        pool.tensor_tensor(ex[:, q % 2, :], ex[:, q % 2, :], sc[:, q // 4 % 2, :],
                                           ALU.mult).then_inc(S("mul_done"), 1)
                zs = n - Z0
                if 0 <= zs < 8:
                    for nb in range(NB):
                        b = NB * zs + nb
                        pool.wait_ge(S("sz_done"), b + 1)
                        pool.wait_ge(S("yadd_done"), b + 1)
                        pool.tensor_tensor(xs[:, b, :], xs[:, b, :], gt[:, nb, :], ALU.mult).then_inc(S("yz_done"), 1)
                if 2 <= zs < 10:
                    for nb in range(NB):
                        lo_part(YS + NB * (zs - 2) + nb)
                if s.kind == "so" and s.last:
                    for nb in range(NB):
                        lo_part(MG + NB * s.j + nb)
                if s.kind == "up" and s.j == 0:
                    for i in range(U2, HID):
                        lo_part(i)
                if s.kind == "up":
                    for nb in range(NB):
                        lo_part(HID + NB * s.j + nb)
                if s.kind == "dq" and s.j == 0:
                    for i in range(U3, MX):
                        lo_part(i)
                if s.kind == "o2" and s.j == 0:
                    for i in range(MX, U4):
                        lo_part(i)
                if s.kind == "gt" and s.j == 0:
                    for i in range(U4, HID2):
                        lo_part(i)
                if s.kind == "u2":
                    for nb in range(NB):
                        lo_part(HID2 + NB * s.j + nb)
                if n in col_at:
                    m = col_at[n]
                    cc = 8 * (m + NB * NA0 >= 48)
                    pool.wait_ge(S("cact"), 1)
                    pool.wait_ge(S(f"col_in{m % 2}"), 16 * (m // 2 + 1))
                    pool.tensor_tensor(colw[:, m % 2, :, :], colw[:, m % 2, :, :],
                                       cact[:, cc:cc + KB].unsqueeze(2).to_broadcast([P, KB, P]), ALU.mult)\
                        .then_inc(S("col_mul"), 1)

        @block.scalar
        def _(act):
            def split_hi(n):
                s = steps[n]
                wait_raw(act, ("step", n))
                if n >= NHL:
                    wait_step(act, n - NHL)
                act.activation(w_hi[:, n % NHL, 0:s.kts, 0:s.cols], raw_of(("step", n), s), ACT.Copy)\
                   .then_inc(S("hi_ready"), 1)

            def hi_part(i, shift=None):
                hi, _ = dest(i)
                x = fr[:, i % NF, :]
                act.wait_ge(S("f_ready"), i + 1)
                if shift is None:
                    act.activation(hi, x, ACT.Copy).then_inc(S("act_hi"), 1)
                else:
                    act.activation(hi, x, ACT.Identity, bias=shift)
                    act.activation(x, x, ACT.Identity, bias=shift).then_inc(S("act_hi"), 1)

            def x_square(i):
                act.wait_ge(S("x_ready"), i + 1)
                if i >= 4:
                    act.wait_ge(S("xsum_done"), i - 3)
                act.activation(sq[:, i % 4, :], xT[:, i % KB, :], ACT.Square).then_inc(S("xsq"), 1)

            def x_root(n):
                act.wait_ge(S("xsum_done"), KB * (n + 1))
                act.activation(rt[:, 0, :], M4[:, 0:T], ACT.Sqrt, bias=eps[:, :], scale=1.0 / D)\
                   .then_inc(S("xroot"), 1)

            def x_norm(n):
                x_root(n)
                if NORM_U[n] is not None:
                    for b in range(KB):
                        hi_part(NORM_U[n] + b, SH[n][:, b:b + 1])

            chain = [0]

            def link(ins):
                chain[0] += 1
                ins.then_inc(S("act_chain"), 1)
                act.wait_ge(S("act_chain"), chain[0])

            def log1p_exp_parts(w, z, k):
                act.wait_ge(S(("dt_z", "fg_z")[k]), NB)
                link(act.activation(w[:, 0, :], z, ACT.Abs))
                act.activation(w[:, 1, :], w[:, 0, :], ACT.Exp, scale=-1.0).then_inc(S("sp_e"), 1)
                act.wait_ge(S("sp_w"), k + 1)
                act.activation(w[:, 3, :], w[:, 2, :], ACT.Ln).then_inc(S("sp_ln"), 1)

            act.wait_ge(S("pc"), N_CONST)
            act.wait_ge(S("par_done"), 1)
            act.activation(cact[:, :], c_cols, ACT.Silu).then_inc(S("cact"), 1)
            for i in range(KB):
                x_square(i)
            split_hi(0)
            split_hi(1)
            act.wait_ge(S("vec_in"), 16 * N_VEC)
            act.activation(nega[:, :], hb[:, 1, :], ACT.Exp).then_inc(S("nega"), 1)
            act.wait_ge(S("lam_dots"), 1)
            act.activation(small[:, 4:6], small[:, 2:4], ACT.Exp).then_inc(S("lam_exp"), 1)
            x_norm(0)

            def attn_tick(m):
                if m < 16:
                    b = m % 2
                    act.wait_ge(S("mx_done"), m + 1)
                    if m == 0:
                        act.wait_ge(S("col_sum"), NCOL)
                    if m >= 2:
                        if product_of(m - 2) is None:
                            act.wait_ge(S("p_done"), m)
                        else:
                            act.wait_ge(S("tr_done"), product_of(m - 2) + 1)
                    act.activation(ex[:, b, 0:P], seg[:, b, 0:P], ACT.Exp, bias=nmx[:, b, 0:1],
                                   accum_out=rs[:, b, 0:1])
                    act.activation(ex[:, b, P:3 * P], seg[:, b, P:3 * P], ACT.Exp, bias=nmx[:, b, 1:2],
                                   accum_out=rs[:, b, 1:2]).then_inc(S("ex_done"), 1)
                c = product_of(m - 2)
                if c is not None:
                    act.wait_ge(S("tr_done"), c + 1)
                    if c >= 2:
                        act.wait_ge(S("pv_done"), c - 1)
                    else:
                        act.wait_ge(S("col_used"), NCOL)
                    act.activation(sc[:, c % 2, :], M3[:, 0:3 * P], ACT.Copy).then_inc(S("pt_done"), 1)
                c = product_of(m - 4)
                if c is not None and c < 4:
                    act.wait_ge(S("o_copied"), c + 1)
                    act.activation(sq[:, 0, :], cv[:, c % 2, :], ACT.Square).then_inc(S("osq"), 1)
                c = product_of(m - 5)
                if c is not None and c < 4:
                    act.wait_ge(S("osum"), c + 1)
                    if c:
                        act.wait_ge(S("f_ready"), MX + c)
                    act.activation(sq[:, 1, :], M0[:, 0:T], ACT.Sqrt, bias=eps[:, :], scale=1.0 / P)\
                       .then_inc(S("oroot"), 1)
                if c is not None and c >= 4 and c % 2:
                    hi_part(MX + 4 + (c - 4) // 2)
                c = product_of(m - 6)
                if c is not None and c < 4:
                    hi_part(MX + c)

            def out_copy(b):
                act.wait_ge(S("otr_done"), b + 1)
                act.activation(outb[:, :, b * P:(b + 1) * P], (M3, M4)[b % 2][:, 0:T].rearrange("p (a c) -> p a c", c=P),
                               ACT.Copy).then_inc(S("out_ready"), 1)

            jq = 0
            for n in range(NS):
                s = steps[n]
                if n + 2 < NS:
                    split_hi(n + 2)
                zs = n - Z0
                if 2 <= zs < 10:
                    act.wait_ge(S("zsum_done"), zs - 1)
                    act.activation(rt[:, 0, :], M3[:, 0:T], ACT.Sqrt, bias=eps[:, :], scale=1.0 / (2 * P))\
                       .then_inc(S("zroot"), 1)
                for nb in range(NB):
                    bank = acc[(s.g + nb) % NACC]
                    ps, free = bank[:, 0:T], S(drained(s, nb)[0])
                    takes = s.last and s.kind in ("xbc", "cc", "gc", "z", "gs", "up", "dq", "dk", "fq", "fk", "fv",
                                                  "dv", "gt")
                    if takes:
                        act.wait_ge(S("acc_ready"), s.g + nb + 1)
                    if s.kind == "xbc":
                        i = NB * s.j + nb
                        fb = (i + 16) % 32
                        if i >= 2:
                            act.wait_ge(S("conv_done"), i - 1)
                            act.wait_ge(S("silu_done"), i - 1)
                        act.activation(stg[:, i % 2, 3:T + 3], ps, ACT.Copy).then_inc(S("stg_ready"), 1)
                        act.activation(cv[:, i % 2, :], ps, ACT.Identity, bias=ssm_b[:, fb:fb + 1],
                                       scale=ssm_w[:, 96 + fb:97 + fb]).then_inc(free, 1)
                    if s.kind == "cc":
                        if s.j:
                            act.wait_ge(S("cx_in"), NB * (s.j - 1) + nb + 1)
                        act.activation(cct[:, nb, :], ps, ACT.Copy).then_inc(free, 1)
                    if s.kind in ("gc", "gs"):
                        c = (4 * (s.kind == "gs") + s.j) * NB + nb
                        if c >= NB:
                            act.wait_ge(S("gate_used"), c - NB + 1)
                        if c >= 8:
                            act.wait_ge(S("yz_done"), 16)
                        act.activation(gt[:, nb, :], ps, ACT.Sigmoid).then_inc(free, 1)
                    if s.kind == "z":
                        i = NB * s.j + nb
                        if i >= 2:
                            act.wait_ge(S("yz_done"), i - 1)
                        else:
                            act.wait_ge(S("gate_used"), 8)
                        act.activation(gt[:, nb, :], ps, ACT.Silu).then_inc(free, 1)
                    if s.kind == "up":
                        i = NB * s.j + nb
                        if i >= 2:
                            act.wait_ge(S("f_ready"), HID + i - 1)
                        act.activation(gt[:, nb, :], ps, ACT.Relu).then_inc(free, 1)
                    if s.kind == "gt":
                        i = NB * s.j + nb
                        if i >= 2:
                            act.wait_ge(S("f_ready"), HID2 + i - 1)
                        act.activation(gt[:, nb, :], ps, ACT.Silu).then_inc(free, 1)
                    if s.kind in ("dq", "dk", "fq", "fk"):
                        b = {"dq": 0, "dk": 4, "fq": 8, "fk": 12}[s.kind] + NB * s.j + nb
                        if nb == 0 and QK_ORDER.index((s.kind, s.j)):
                            act.wait_ge(S("qsum_done"), QK_ORDER.index((s.kind, s.j)))
                        act.activation(sq[:, 2 + nb, :], ps, ACT.Square).then_inc(S("qsq"), 1)
                        act.activation(qk[:, b, :], ps, ACT.Copy).then_inc(free, 1)
                    if s.kind == "d2" and s.k == 0 and s.j:
                        out_copy(NB * (s.j - 1) + nb)
                    if s.kind in ("fv", "dv"):
                        o = (4 * (s.kind == "dv")) * P + s.j * CW
                        act.activation(v[:, nb, o:o + CW], ps, ACT.Copy).then_inc(free, 1)
                    prev = steps[n - 1].kind if n else ""
                    if nb == 0 and prev in ("dq", "dk", "fq", "fk"):
                        jq += 1
                        act.wait_ge(S("qsum_done"), jq)
                        if jq > 1:
                            act.wait_ge(S("qk_done"), NB * (jq - 1))
                        act.activation(rt[:, :, :].rearrange("p a b -> p (a b)"), M0[:, :], ACT.Sqrt, bias=eps[:, :],
                                       scale=1.0 / HD).then_inc(S("qroot"), 1)
                    if X0 <= n and NB * (n - X0) + nb - 1 in range(32):
                        i = NB * (n - X0) + nb - 1
                        fb = (i + 16) % 32
                        dst = xs[:, fb, :] if fb < 16 else bct[:, fb - 16, :]
                        act.wait_ge(S("conv_done"), i + 1)
                        act.activation(dst, cv[:, i % 2, :], ACT.Silu).then_inc(S("silu_done"), 1)
                    if s.kind == "cb":
                        hi_part(YC + NB * s.j + nb)
                    if s.kind == "so" and s.last:
                        hi_part(MG + NB * s.j + nb)
                    if s.kind == "up":
                        hi_part(HID + NB * s.j + nb)
                    if s.kind == "u2":
                        hi_part(HID2 + NB * s.j + nb)
                    for kind, norm in (("wo", 1), ("dn", 2), ("o2", 4)):
                        if s.kind == kind and s.last:
                            x_square(KB * norm + NB * s.j + nb)
                    q = NB * (n - SCAN0) + nb
                    if 0 <= q < HEADS:
                        if q % 4 == 0:
                            g = q // 4
                            act.wait_ge(S("scores"), g + 1)
                            if g == 0:
                                act.wait_ge(S("col_used"), XCOL)
                            if g >= 2:
                                act.wait_ge(S("mul_done"), 4 * (g - 1))
                            act.activation(sc[:, g % 2, :], M3[:, 0:3 * P], ACT.Copy).then_inc(S("sc_done"), 1)
                        act.wait_ge(S("seg_done"), q + 1)
                        if q >= 2:
                            act.wait_ge(S("y_done"), q - 1)
                        act.activation(ex[:, q % 2, :], seg[:, q % 2, :], ACT.Exp).then_inc(S("exp_done"), 1)
                    if n >= I0 + 7 and NB * (n - I0 - 7) + nb < 12:
                        attn_tick(NB * (n - I0 - 7) + nb)
                if s.kind == "dt":
                    log1p_exp_parts(dtr[:, 1:6, :], dtr[:, 0, :], 0)
                if s.kind == "fg":
                    log1p_exp_parts(dtr[:, 1:6, 0:16], dtr[:, 0, 0:16], 1)
                if 1 <= zs < 9:
                    for nb in range(NB):
                        act.wait_ge(S("yz_done"), NB * (zs - 1) + nb + 1)
                        if zs >= 3:
                            act.wait_ge(S("zsum_done"), zs - 2)
                        act.activation(sq[:, 2 * (zs % 2) + nb, :], xs[:, NB * (zs - 1) + nb, :],
                                       ACT.Square).then_inc(S("zsq"), 1)
                if 2 <= zs < 10:
                    for nb in range(NB):
                        hi_part(YS + NB * (zs - 2) + nb)
                if s.kind == "wo" and s.j == 3:
                    x_norm(1)
                if s.kind == "dn" and s.j == 3 and s.last:
                    x_norm(2)
                    for i in range(KB):
                        x_square(3 * KB + i)
                    x_norm(3)
                if s.kind == "fv" and s.j == 1:
                    for m in range(12, 21):
                        attn_tick(m)
                if s.kind == "o2" and s.j == 3:
                    x_norm(4)
            out_copy(KB - 2)
            out_copy(KB - 1)


        @block.tensor
        def _(pe):
            free = {}

            def take(bank):
                if bank in free:
                    pe.wait_ge(S(free[bank][0]), free[bank][1])

            pe.wait_ge(S("pc"), N_CONST)
            pe.wait_ge(S("par_in"), 16 * N_PAR)
            for i, bank in enumerate((M1, M2, M3)):
                pe.transpose(bank[:, 0:P], rows[:, i, :], ident[:, :]).then_inc(S("par_t"), 1)
            free["M1"] = free["M2"] = free["M3"] = ("par_done", 1)
            pe.wait_ge(S("x_in"), 16)
            for b in range(KB):
                name, bank = (("M1", M1), ("M2", M2), ("M3", M3))[b % 3]
                take(name)
                for t in range(TT):
                    ins = pe.transpose(bank[:, t * P:(t + 1) * P], xdt[:, t, b * P:(b + 1) * P], ident[:, :])
                ins.then_inc(S("xt_done"), 1)
                free[name] = ("x_ready", b + 1)

            def x_sum(i):
                b = i % KB
                if b == 0:
                    take("M4")
                pe.wait_ge(S("xsq"), i + 1)
                pe.matmul(M4[:, 0:T], ones[:, :], sq[:, i % 4, :], start=(b == 0), stop=(b == KB - 1))\
                  .then_inc(S("xsum_done"), 1)
                if b == KB - 1:
                    free["M4"] = ("xroot", i // KB + 1)

            for i in range(KB):
                x_sum(i)

            def ada(n):
                wait_raw(pe, ("ada", n))
                w = raw_of(("ada", n))
                for nb in range(NB):
                    col = NB * n + nb
                    for k in range(KB):
                        ins = pe.matmul(M0[:, col:col + 1], w[:, k, nb * P:(nb + 1) * P], cact[:, k:k + 1],
                                        start=(k == 0), stop=(k == KB - 1))
                ins.then_inc(S("ada_used"), 1)

            def ada_column(m):
                col = m + NB * NA0
                if m == 0:
                    pe.wait_ge(S("mod_done"), 1)
                pe.wait_ge(S("col_sum"), m + 1)
                if col == 64:
                    take("M3")
                    free["M3"] = ("mod_done", 5)
                pe.matmul(mod_bank(col)[:, col:col + 1], cols[:, m % 2, :], ones[:, 0:1], start=True, stop=True)\
                  .then_inc(S("col_used"), 1)

            pe.wait_ge(S("cact"), 1)
            for n in range(NA0):
                ada(n)

            def product(n, nb):
                s = steps[n]
                g = s.g + nb
                H, L = operands(s.act)
                out_ = acc[g % NACC]
                if nb == 0:
                    pe.wait_ge(S("lo_ready"), n + 1)
                if s.k == 0 and g >= NACC:
                    name, value = drained(*block_of[g - NACC])
                    pe.wait_ge(S(name), value)
                for kt in range(s.kts):
                    need = U4 if s.act == MX else s.act + s.kt0 + kt + 1
                    if need > seen[0]:
                        pe.wait_ge(S("act_lo"), need)
                        seen[0] = need
                    x_hi, x_lo = H[:, s.kt0 + kt, :], L[:, s.kt0 + kt, :]
                    wh, wl = w_hi[:, n % NHL, kt, 0:s.cols], w_lo[:, n % NHL, kt, 0:s.cols]
                    if s.tokens_out:
                        o = out_[:, 0:s.cols]
                        x_hi, x_lo = x_hi[:, nb * P:(nb + 1) * P], x_lo[:, nb * P:(nb + 1) * P]
                        pairs = ((x_hi, wh), (x_hi, wl), (x_lo, wh))
                    else:
                        o = out_[:, 0:T]
                        wh, wl = wh[:, nb * P:(nb + 1) * P], wl[:, nb * P:(nb + 1) * P]
                        pairs = ((wh, x_hi), (wh, x_lo), (wl, x_hi))
                    for i, (l, r) in enumerate(pairs):
                        ins = pe.matmul(o, l, r, start=(s.k == 0 and kt == 0 and i == 0),
                                        stop=(s.last and kt == s.kts - 1 and i == 2))
                if s.last:
                    ins.then_inc(S("acc_ready"), 1)
                elif nb == NB - 1:
                    ins.then_inc(S("part_done"), 1)

            seen = [0]
            block_of = [(s_, nb_) for s_ in steps if s_.k == 0 for nb_ in range(NB)]

            def scan_slot(q):
                if q % 4 == 0 and q < HEADS:
                    g = q // 4
                    if g == 0:
                        pe.wait_ge(S("silu_done"), 32)
                    take("M3")
                    B, C = bct[:, g, :], bct[:, GROUPS + g, :]
                    pe.matmul(M3[:, 0:T], B[:, 0:P], C, start=True, stop=True)
                    pe.matmul(M3[:, T:T + P], B[:, P:T], C[:, P:T], start=True, stop=True).then_inc(S("scores"), 1)
                    free["M3"] = ("sc_done", g + 1)
                if q < HEADS:
                    bank = (M1, M2)[q % 2]
                    if q >= 2:
                        pe.wait_ge(S("seg_done"), q - 1)
                    pe.matmul(bank[:, 0:T], dta[:, 0, q:q + 1].to_broadcast([P, P]), tri[:, :], start=True, stop=False)
                    pe.matmul(bank[:, P:T], dta[:, 1, q:q + 1].to_broadcast([P, P]), tri[:, 0:P], start=False,
                              stop=True).then_inc(S("bc_done"), 1)
                h = q - 2
                if 0 <= h < HEADS:
                    o = HD * (h % 2)
                    pe.wait_ge(S("mul_done"), h + 1)
                    if h % 2 == 0:
                        take("M4")
                    pe.matmul(M4[o:o + HD, 0:T], xdt[:, 0, h * HD:(h + 1) * HD], ex[:, h % 2, 0:T], start=True,
                              stop=False)
                    pe.matmul(M4[o:o + HD, P:T], xdt[:, 1, h * HD:(h + 1) * HD], ex[:, h % 2, T:T + P], start=False,
                              stop=True).then_inc(S("y_done"), 1)
                    if h % 2:
                        free["M4"] = ("yadd_done", h // 2 + 1)

            def x_transpose(i):
                bank = ("M3", "M4")[i % 2]
                pe.wait_ge(S("silu_done"), 16 + i + 1)
                take(bank)
                b = (M3, M4)[i % 2]
                for t in range(TT):
                    ins = pe.transpose(b[:, t * P:(t + 1) * P], xs[:, i, t * P:(t + 1) * P], ident[:, :])
                ins.then_inc(S("xs_t"), 1)
                free[bank] = ("xdt_done", i + 1)

            def attn_tick(m):
                if m < 16:
                    bank = (M1, M2)[m % 2]
                    if m >= 2:
                        pe.wait_ge(S("l_done"), m - 1)
                    if m == 0:
                        pe.wait_ge(S("qk_done"), 8)
                    if m == 8:
                        pe.wait_ge(S("qk_done"), 12)
                    if m == 12:
                        pe.wait_ge(S("qk_done"), 16)
                    if m < 8:
                        qb, kb, o = m // 2, 4 + m // 2, HD * (m % 2)
                    else:
                        qb, kb, o = 8 + (m - 8) // 2, 12 + (m - 8) // 2, HD * (m % 2)
                    q, k = qk[o:o + HD, qb, :], qk[o:o + HD, kb, :]
                    pe.matmul(bank[:, 0:P], q[:, 0:P], k[:, 0:P], start=True, stop=True)
                    pe.matmul(bank[:, P:3 * P], q[:, P:T], k, start=True, stop=True).then_inc(S("s_done"), 1)
                    if m >= 8:
                        f = m - 8
                        if f == 0:
                            pe.wait_ge(S("lf_done"), 1)
                        take("M0")
                        pe.matmul(M0[:, 0:T], lf[:, 0, f:f + 1].to_broadcast([P, P]), tri[:, :], start=True, stop=False)
                        pe.matmul(M0[:, P:T], lf[:, 1, f:f + 1].to_broadcast([P, P]), tri[:, 0:P], start=False,
                                  stop=True).then_inc(S("fbc_done"), 1)
                        free["M0"] = ("nb_done", f + 1)
                c = product_of(m - 2)
                if c is not None:
                    e = ex[:, m % 2, :]
                    pe.wait_ge(S("p_done"), m - 1)
                    take("M3")
                    pe.transpose(M3[:, 0:P], e[:, 0:P], ident[:, :])
                    pe.transpose(M3[:, P:2 * P], e[:, P:2 * P], ident[:, :])
                    pe.transpose(M3[:, 2 * P:3 * P], e[:, 2 * P:3 * P], ident[:, :]).then_inc(S("tr_done"), 1)
                    free["M3"] = ("pt_done", c + 1)
                c = product_of(m - 3)
                if c is not None:
                    pe.wait_ge(S("pt_done"), c + 1)
                    pt = sc[:, c % 2, :]
                    if c < 4:
                        lo_, n_, o = 512 + c * P, P, 0
                    else:
                        lo_, n_, o = (c - 4) * HD, HD, HD * (c % 2)
                    if c < 4 or c % 2 == 0:
                        take("M4")
                    pe.matmul(M4[o:o + n_, 0:T], v[:, 0, lo_:lo_ + n_], pt[:, 0:T], start=True, stop=False)
                    pe.matmul(M4[o:o + n_, P:T], v[:, 1, lo_:lo_ + n_], pt[:, T:T + P], start=False, stop=True)\
                      .then_inc(S("pv_done"), 1)
                    if c < 4:
                        free["M4"] = ("o_copied", c + 1)
                    elif c % 2:
                        free["M4"] = ("f_ready", MX + 4 + (c - 4) // 2 + 1)
                c = product_of(m - 5)
                if c is not None and c < 4:
                    pe.wait_ge(S("osq"), c + 1)
                    take("M0")
                    pe.matmul(M0[:, 0:T], ones[:, :], sq[:, 0, :], start=True, stop=True).then_inc(S("osum"), 1)
                    free["M0"] = ("oroot", c + 1)

            def out_transpose(b):
                bank = ("M3", "M4")[b % 2]
                take(bank)
                pe.wait_ge(S("x_ready"), 5 * KB + b + 1)
                t_ = (M3, M4)[b % 2]
                for t in range(TT):
                    ins = pe.transpose(t_[:, t * P:(t + 1) * P], xT[:, b, t * P:(t + 1) * P], ident[:, :])
                ins.then_inc(S("otr_done"), 1)
                free[bank] = ("out_ready", b + 1)

            free["M0"] = ("mod_done", 2)
            jq = 0
            for n in range(NS):
                s = steps[n]
                for nb in range(NB):
                    product(n, nb)
                    if n == X0 + 2 and nb == 0:
                        pe.wait_ge(S("dta_done"), 1)
                        take("M3")
                        for t in range(TT):
                            o = M3[:, t * HEADS:(t + 1) * HEADS]
                            if t:
                                pe.matmul(o, ones[:, :], dta[:, 0, :], start=True, stop=False)
                            ins = pe.matmul(o, tri[:, 0:P], dta[:, t, :], start=(t == 0), stop=True)
                        ins.then_inc(S("ac_done"), 1)
                        free["M3"] = ("nac_done", 1)
                    slot = NB * (n - X0) + nb
                    if 18 <= slot < 34:
                        x_transpose(slot - 18)
                    if 0 <= NB * (n - SCAN0) + nb < HEADS + 2:
                        scan_slot(NB * (n - SCAN0) + nb)
                    for kind, norm in (("wo", 1), ("o2", 4)):
                        if s.kind == kind and NB * s.j + nb:
                            x_sum(KB * norm + NB * s.j + nb - 1)
                    if s.kind == "dn" and s.k == 0 and s.j:
                        x_sum(KB * 2 + NB * (s.j - 1) + nb)
                    if nb == 0 and n and steps[n - 1].kind in ("dq", "dk", "fq", "fk"):
                        take("M0")
                        pe.wait_ge(S("qsq"), NB * (jq + 1))
                        for i in range(NB):
                            ins = pe.matmul(M0[:, i * T:(i + 1) * T], blk64[:, :], sq[:, 2 + i, :], start=True, stop=True)
                        jq += 1
                        ins.then_inc(S("qsum_done"), 1)
                        free["M0"] = ("qroot", jq)
                    if n >= I0 + 7 and NB * (n - I0 - 7) + nb < 12:
                        attn_tick(NB * (n - I0 - 7) + nb)
                    if s.kind == "d2" and s.k == 0 and s.j:
                        out_transpose(NB * (s.j - 1) + nb)
                    if s.kind == "fq" and s.j == 0 and nb == 1:
                        pe.wait_ge(S("lf_done"), 1)
                        take("M0")
                        for t in range(TT):
                            o = M0[:, t * 8:(t + 1) * 8]
                            if t:
                                pe.matmul(o, ones[:, :], lf[:, 0, :], start=True, stop=False)
                            ins = pe.matmul(o, tri[:, 0:P], lf[:, t, :], start=(t == 0), stop=True)
                        ins.then_inc(S("fc_done"), 1)
                        free["M0"] = ("fcum_done", 1)
                zs = n - Z0
                if 1 <= zs < 9:
                    take("M3")
                    pe.wait_ge(S("zsq"), NB * zs)
                    for i in range(NB):
                        ins = pe.matmul(M3[:, 0:T], ones[:, :], sq[:, 2 * (zs % 2) + i, :], start=(i == 0), stop=(i == 1))
                    ins.then_inc(S("zsum_done"), 1)
                    free["M3"] = ("zroot", zs)
                if n - 2 in col_at:
                    ada_column(col_at[n - 2])
                if s.kind == "wo" and s.j == 3:
                    x_sum(2 * KB - 1)
                if s.kind == "dn" and s.j == 3 and s.last:
                    x_sum(3 * KB - 2)
                    x_sum(3 * KB - 1)
                    for b in range(KB):
                        x_sum(3 * KB + b)
                if s.kind == "fv" and s.j == 1:
                    for m in range(12, 21):
                        attn_tick(m)
                if s.kind == "o2" and s.j == 3:
                    x_sum(5 * KB - 1)
            out_transpose(KB - 2)
            out_transpose(KB - 1)

        @block.vector
        def _(dve):
            chain = [0]

            def link(ins):
                chain[0] += 1
                ins.then_inc(S("dve_chain"), 1)
                dve.wait_ge(S("dve_chain"), chain[0])

            def split_lo(n):
                s = steps[n]
                dve.wait_ge(S("hi_ready"), n + 1)
                hi, lo = (w[:, n % NHL, 0:s.kts, 0:s.cols] for w in (w_hi, w_lo))
                dve.tensor_tensor(lo, raw_of(("step", n), s), hi.bitcast(F32), ALU.subtract).then_inc(S("lo_ready"), 1)

            def f_slot(i):
                if i >= NF:
                    dve.wait_ge(S("act_lo"), i - NF + 1)
                return fr[:, i % NF, :]

            def take_mod(c0, c1):
                if c1 <= NB * NA0:
                    dve.wait_ge(S("ada_used"), NA0)
                else:
                    dve.wait_ge(S("col_used"), c1 - NB * NA0)
                dve.tensor_tensor(mod[:, c0:c1], mod_bank(c0)[:, c0:c1], ada_b[:, c0:c1], ALU.add)\
                   .then_inc(S("mod_done"), 1)

            def make_gain(n):
                link(dve.scalar_tensor_tensor(gain[:, n, :], SCL[n], 1.0, LN[n], ALU.add, ALU.mult))

            def x_norm(n):
                dve.wait_ge(S("xroot"), n + 1)
                link(dve.reciprocal(rb[:, 0, :], rt[:, 0, :]))
                for b in range(KB):
                    if NORM_U[n] is None:
                        dve.scalar_tensor_tensor(xT[:, b, :], xT[:, b, :], final_w[:, b:b + 1], rb[:, 0, :], ALU.mult,
                                                 ALU.mult).then_inc(S("x_ready"), 1)
                    else:
                        i = NORM_U[n] + b
                        dve.scalar_tensor_tensor(f_slot(i), xT[:, b, :], gain[:, n, b:b + 1], rb[:, 0, :], ALU.mult,
                                                 ALU.mult).then_inc(S("f_ready"), 1)

            def softplus(w, z, k, sign):
                dve.wait_ge(S("sp_e"), k + 1)
                link(dve.tensor_scalar(w[:, 2, :], w[:, 1, :], 1.0, None, ALU.add))
                dve.tensor_scalar(w[:, 4, :], w[:, 2, :], -1.0, None, ALU.add).then_inc(S("sp_w"), 1)
                dve.wait_ge(S("sp_w"), k + 1)
                link(dve.tensor_tensor(w[:, 4, :], w[:, 1, :], w[:, 4, :], ALU.subtract))
                link(dve.reciprocal(w[:, 0, :], w[:, 2, :]))
                link(dve.tensor_tensor(w[:, 4, :], w[:, 4, :], w[:, 0, :], ALU.mult))
                dve.wait_ge(S("sp_ln"), k + 1)
                link(dve.tensor_tensor(w[:, 4, :], w[:, 4, :], w[:, 3, :], ALU.add))
                link(dve.tensor_scalar(w[:, 0, :], z, sign, 0.0, ALU.mult, ALU.max))
                link(dve.tensor_tensor(w[:, 4, :], w[:, 4, :], w[:, 0, :], ALU.add))

            dve.wait_ge(S("pc"), N_CONST)
            dve.wait_ge(S("par_t"), 3)
            for i, bank in enumerate((M1, M2, M3)):
                ins = dve.tensor_copy(par[:, i, :], bank[:, 0:P])
            ins.then_inc(S("par_done"), 1)
            for b in range(KB):
                dve.wait_ge(S("xt_done"), b + 1)
                dve.tensor_copy(xT[:, b, :], (M1, M2, M3)[b % 3][:, 0:T]).then_inc(S("x_ready"), 1)
            dve.wait_ge(S("vec_in"), 16 * N_VEC)
            link(dve.tensor_tensor(lamw[:, 0, :], lamw[:, 0, :], lamw[:, 1, :], ALU.mult))
            link(dve.tensor_tensor(lamw[:, 2, :], lamw[:, 2, :], lamw[:, 3, :], ALU.mult))
            dve.tensor_reduce(small[:, 2:3], lamw[:, 0, :], AX_X, ALU.add)
            dve.tensor_reduce(small[:, 3:4], lamw[:, 2, :], AX_X, ALU.add).then_inc(S("lam_dots"), 1)
            split_lo(0)
            split_lo(1)
            dve.wait_ge(S("par_done"), 1)
            link(dve.tensor_scalar(small[:, 6:7], qk_gain[:, 0:1], HD ** -0.5, None, ALU.mult))
            link(dve.tensor_scalar(small[:, 7:8], qk_gain[:, 2:3], HD ** -0.5, None, ALU.mult))
            link(dve.tensor_scalar(small[:, 8:9], dn_gain, 1.0 - LAM_INIT, None, ALU.mult))
            dve.wait_ge(S("lam_exp"), 1)
            link(dve.tensor_tensor(small[:, 1:2], small[:, 5:6], small[:, 4:5], ALU.subtract))
            link(dve.tensor_scalar(small[:, 0:1], small[:, 1:2], -LAM_INIT, None, ALU.add))
            for half in range(2):
                link(dve.tensor_copy(dsk[half * HD:(half + 1) * HD, :], hb[half * HD:(half + 1) * HD, 2, half:HEADS:2]))
            dve.wait_ge(S("nega"), 1)
            link(dve.tensor_scalar(nega[:, :], nega[:, :], -1.0, None, ALU.mult))
            take_mod(0, NB * NA0)
            dve.wait_ge(S("mod_done"), 1)
            make_gain(0)
            x_norm(0)

            def seg_slot(q):
                if q < HEADS:
                    bank = (M1, M2)[q % 2]
                    dve.wait_ge(S("bc_done"), q + 1)
                    if q >= 2:
                        dve.wait_ge(S("exp_done"), q - 1)
                    dve.scalar_tensor_tensor(seg[:, q % 2, 0:T], bank[:, 0:T], nac[:, 0, q:q + 1], min_st[:, :],
                                             ALU.add, ALU.min)
                    dve.scalar_tensor_tensor(seg[:, q % 2, T:T + P], bank[:, P:T], nac[:, 1, q:q + 1], min_st[:, 0:P],
                                             ALU.add, ALU.min).then_inc(S("seg_done"), 1)
                if q >= 3 and q % 2:
                    p = (q - 3) // 2
                    dve.wait_ge(S("y_done"), 2 * p + 2)
                    dve.scalar_tensor_tensor(xs[:, p, :], xs[:, p, :], dsk[:, p:p + 1], M4[:, 0:T], ALU.mult,
                                             ALU.add).then_inc(S("yadd_done"), 1)

            def attn_tick(m):
                c = product_of(m - 6)
                if c is not None and c < 4:
                    dve.wait_ge(S("oroot"), c + 1)
                    link(dve.reciprocal(sq[:, 1, :], sq[:, 1, :]))
                    dve.scalar_tensor_tensor(f_slot(MX + c), cv[:, c % 2, :], small[:, 8:9], sq[:, 1, :], ALU.mult,
                                             ALU.mult).then_inc(S("f_ready"), 1)
                w = m - 1
                if 0 <= w < 16:
                    b = w % 2
                    e = ex[:, b, :]
                    dve.wait_ge(S("ex_done"), w + 1)
                    link(dve.reciprocal(rr[:, b, :], rs[:, b, :]))
                    if w < 8 and b == 1:
                        link(dve.tensor_scalar(rr[:, b, :], rr[:, b, :], NEG_LAM, None, ALU.mult))
                        link(dve.scalar_tensor_tensor(e[:, 0:P], e[:, 0:P], rr[:, b, 0:1], ex[:, 0, 0:P], ALU.mult,
                                                      ALU.add))
                        dve.scalar_tensor_tensor(e[:, P:3 * P], e[:, P:3 * P], rr[:, b, 1:2], ex[:, 0, P:3 * P],
                                                 ALU.mult, ALU.add).then_inc(S("p_done"), 1)
                    else:
                        link(dve.tensor_scalar(e[:, 0:P], e[:, 0:P], rr[:, b, 0:1], None, ALU.mult))
                        dve.tensor_scalar(e[:, P:3 * P], e[:, P:3 * P], rr[:, b, 1:2], None, ALU.mult)\
                           .then_inc(S("p_done"), 1)
                        dve.wait_ge(S("p_done"), w + 1)
                if m < 16:
                    b = m % 2
                    bank = (M1, M2)[b]
                    L = seg[:, b, :]
                    dve.wait_ge(S("s_done"), m + 1)
                    if m < 8:
                        slope = 2.0 ** (-8.0 * (m // 2 + 1) / 4)
                        link_l(dve.scalar_tensor_tensor(L, dist_ts[:, :], slope, bank[:, 0:3 * P], ALU.mult, ALU.add), m)
                    else:
                        f = m - 8
                        dve.wait_ge(S("fbc_done"), f + 1)
                        dve.tensor_tensor(L[:, 0:P], mask_ts[:, 0:P], M0[:, 0:P], ALU.subtract)
                        dve.tensor_tensor(L[:, P:3 * P], mask_ts[:, P:3 * P], M0[:, 0:T], ALU.subtract)\
                           .then_inc(S("nb_done"), 1)
                        dve.wait_ge(S("nb_done"), f + 1)
                        link(dve.scalar_tensor_tensor(L[:, 0:P], bank[:, 0:P], fcum[:, 0, f:f + 1], L[:, 0:P], ALU.add,
                                                      ALU.add))
                        link_l(dve.scalar_tensor_tensor(L[:, P:3 * P], bank[:, P:3 * P], fcum[:, 1, f:f + 1],
                                                        L[:, P:3 * P], ALU.add, ALU.add), m)
                    dve.tensor_reduce(nmx[:, b, 0:1], L[:, 0:P], AX_X, ALU.max, negate=True)
                    dve.tensor_reduce(nmx[:, b, 1:2], L[:, P:3 * P], AX_X, ALU.max, negate=True).then_inc(S("mx_done"), 1)
                c = product_of(m - 4)
                if c is not None and c < 4:
                    dve.wait_ge(S("pv_done"), c + 1)
                    dve.tensor_copy(cv[:, c % 2, :], M4[:, 0:T]).then_inc(S("o_copied"), 1)
                if c is not None and c >= 4 and c % 2:
                    dve.wait_ge(S("pv_done"), c + 1)
                    dve.tensor_copy(f_slot(MX + 4 + (c - 4) // 2), M4[:, 0:T]).then_inc(S("f_ready"), 1)

            def link_l(ins, m):
                ins.then_inc(S("l_done"), 1)
                dve.wait_ge(S("l_done"), m + 1)

            jq = 0
            for n in range(NS):
                s = steps[n]
                if n + 2 < NS:
                    split_lo(n + 2)
                if n == MOD1_AT:
                    take_mod(NB * NA0, NB * NA0 + XCOL)
                    take_mod(NB * NA0 + XCOL, 48)
                    dve.wait_ge(S("mod_done"), 3)
                    make_gain(1)
                if n == MOD2_AT:
                    take_mod(48, 64)
                    dve.wait_ge(S("mod_done"), 4)
                    make_gain(3)
                if n == MOD3_AT:
                    take_mod(64, 96)
                    dve.wait_ge(S("mod_done"), 5)
                    make_gain(4)
                for nb in range(NB):
                    bank = acc[(s.g + nb) % NACC]
                    ps, free = bank[:, 0:T], S(drained(s, nb)[0])
                    ready = lambda: dve.wait_ge(S("acc_ready"), s.g + nb + 1)
                    if s.kind == "dt":
                        ready()
                        dve.tensor_tensor(dtr[:, 0, nb * HEADS:(nb + 1) * HEADS], bank[:, 0:HEADS], hb[:, 0, :],
                                          ALU.add).then_inc(free, 1)
                    if s.kind == "fg":
                        ready()
                        dve.tensor_tensor(dtr[:, 0, nb * 8:(nb + 1) * 8], bank[:, 0:8], bf[:, :], ALU.add).then_inc(free, 1)
                    if s.kind == "xbc":
                        i = NB * s.j + nb
                        fb = (i + 16) % 32
                        dve.wait_ge(S("stg_ready"), i + 1)
                        dve.wait_ge(free, i + 1)
                        for tap in (2, 1, 0):
                            ins = dve.scalar_tensor_tensor(cv[:, i % 2, :], stg[:, i % 2, tap:tap + T],
                                                           ssm_w[:, 32 * tap + fb:32 * tap + fb + 1], cv[:, i % 2, :],
                                                           ALU.mult, ALU.add)
                            if tap:
                                link(ins)
                        ins.then_inc(S("conv_done"), 1)
                    slot = NB * (n - X0) + nb
                    if 18 <= slot < 34:
                        i = slot - 18
                        dve.wait_ge(S("xs_t"), i + 1)
                        dve.tensor_tensor(xdt[:, :, i * P:(i + 1) * P].rearrange("p t (h d) -> p t h d", d=HD),
                                          (M3, M4)[i % 2][:, 0:T].rearrange("p (t h d) -> p t h d", t=TT, d=HD),
                                          dt_sb[:, :, 2 * i:2 * i + 2].unsqueeze(3).to_broadcast([P, TT, 2, HD]),
                                          ALU.mult).then_inc(S("xdt_done"), 1)
                    if s.kind == "cx":
                        ready()
                        if s.j == 0 and nb == 0:
                            dve.wait_ge(S("silu_done"), 32)
                        b = NB * s.j + nb
                        dve.wait_ge(S("cc_out"), b + 1)
                        dve.tensor_tensor(stg[:, nb, 3:T + 3], ps, cct[:, nb, :], ALU.mult).then_inc(free, 1)
                        dve.wait_ge(free, b + 1)
                        link(dve.tensor_scalar(cv[:, nb, :], stg[:, nb, 3:T + 3], conv_w[:, 16 + b:17 + b], None, ALU.mult))
                        link(dve.scalar_tensor_tensor(cv[:, nb, :], stg[:, nb, 2:T + 2], conv_w[:, 8 + b:9 + b],
                                                      cv[:, nb, :], ALU.mult, ALU.add))
                        dve.scalar_tensor_tensor(cv[:, nb, :], stg[:, nb, 1:T + 1], conv_w[:, b:b + 1], cv[:, nb, :],
                                                 ALU.mult, ALU.add).then_inc(S("cx_done"), 1)
                    if s.kind == "cb":
                        ready()
                        i = YC + NB * s.j + nb
                        f = f_slot(i)
                        dve.wait_ge(S("cx_done"), NB * s.j + nb + 1)
                        dve.tensor_tensor(f, ps, cv[:, nb, :], ALU.mult).then_inc(S("f_ready"), 1)
                    if s.kind == "co":
                        ready()
                        dve.wait_ge(S("gate"), NB * s.j + nb + 1)
                        dve.tensor_tensor(mc[:, NB * s.j + nb, :], ps, gt[:, nb, :], ALU.mult).then_inc(S("gate_used"), 1)
                    if s.kind == "so" and s.last:
                        ready()
                        dve.wait_ge(S("gate"), 8 + NB * s.j + nb + 1)
                        dve.tensor_tensor(cv[:, nb, :], ps, gt[:, nb, :], ALU.mult).then_inc(S("gate_used"), 1)
                        dve.wait_ge(S("gate_used"), 8 + NB * s.j + nb + 1)
                        i = MG + NB * s.j + nb
                        dve.tensor_tensor(f_slot(i), cv[:, nb, :], mc[:, NB * s.j + nb, :], ALU.add)\
                           .then_inc(S("f_ready"), 1)
                    for kind, gate in (("wo", 0), ("dn", 1), ("o2", 2), ("d2", 3)):
                        if s.kind == kind and s.last:
                            ready()
                            b = NB * s.j + nb
                            dve.scalar_tensor_tensor(xT[:, b, :], ps, GATE[gate][:, b:b + 1], xT[:, b, :], ALU.mult,
                                                     ALU.add).then_inc(S("x_ready"), 1)
                    if s.kind == "up":
                        i = HID + NB * s.j + nb
                        dve.wait_ge(S("relu"), NB * s.j + nb + 1)
                        dve.tensor_tensor(f_slot(i), gt[:, nb, :], gt[:, nb, :], ALU.mult).then_inc(S("f_ready"), 1)
                    if s.kind == "u2":
                        i = HID2 + NB * s.j + nb
                        ready()
                        dve.wait_ge(S("silu_g"), NB * s.j + nb + 1)
                        dve.tensor_tensor(f_slot(i), ps, gt[:, nb, :], ALU.mult).then_inc(S("f_ready"), 1)
                    q = NB * (n - SCAN0) + nb
                    if 0 <= q < HEADS + 2:
                        seg_slot(q)
                    prev = steps[n - 1] if n else None
                    if nb == 0 and prev and prev.kind in ("dq", "dk", "fq", "fk"):
                        jq += 1
                        dve.wait_ge(S("qroot"), jq)
                        link(dve.reciprocal(rb[:, :, :].rearrange("p a b -> p (a b)"), rt[:, :, :].rearrange("p a b -> p (a b)")))
                        base, gcol = {"dq": (0, small[:, 7:8]), "dk": (4, qk_gain[:, 3:4]), "fq": (8, small[:, 6:7]),
                                      "fk": (12, qk_gain[:, 1:2])}[prev.kind]
                        for half in range(NB):
                            b = base + NB * prev.j + half
                            dve.scalar_tensor_tensor(qk[:, b, :], qk[:, b, :], gcol, rb[:, half, :], ALU.mult, ALU.mult)\
                               .then_inc(S("qk_done"), 1)
                    if n >= I0 + 7 and NB * (n - I0 - 7) + nb < 12:
                        attn_tick(NB * (n - I0 - 7) + nb)
                    if s.kind == "fq" and s.j == 0 and nb == 1:
                        dve.wait_ge(S("fc_done"), 1)
                        dve.tensor_copy(fcum[:, :, :].rearrange("p a b -> p (a b)"), M0[:, 0:16]).then_inc(S("fcum_done"), 1)
                    if n == X0 + 2 and nb == 0:
                        dve.wait_ge(S("ac_done"), 1)
                        dve.tensor_scalar(nac[:, :, :].rearrange("p a b -> p (a b)"), M3[:, 0:TT * HEADS], -1.0, None,
                                          ALU.mult).then_inc(S("nac_done"), 1)
                if s.kind == "dt":
                    softplus(dtr[:, 1:6, :], dtr[:, 0, :], 0, 1.0)
                    flat = lambda t_: t_[:, :, :].rearrange("p a b -> p (a b)")
                    link(dve.tensor_copy(flat(dt_sb), dtr[:, 5, :]))
                    dve.tensor_tensor(dta[:, :, :], dt_sb[:, :, :], nega[:, :].unsqueeze(1).to_broadcast([P, TT, HEADS]),
                                      ALU.mult).then_inc(S("dta_done"), 1)
                if s.kind == "fg":
                    softplus(dtr[:, 1:6, 0:16], dtr[:, 0, 0:16], 1, -1.0)
                    dve.tensor_scalar(lf[:, :, :].rearrange("p a b -> p (a b)"), dtr[:, 5, 0:16], -1.0, None,
                                      ALU.mult).then_inc(S("lf_done"), 1)
                zs = n - Z0
                if 2 <= zs < 10:
                    dve.wait_ge(S("zroot"), zs - 1)
                    link(dve.reciprocal(rb[:, 0, :], rt[:, 0, :]))
                    for nb in range(NB):
                        b = NB * (zs - 2) + nb
                        dve.scalar_tensor_tensor(f_slot(YS + b), xs[:, b, :], norm_w[:, b:b + 1], rb[:, 0, :], ALU.mult,
                                                 ALU.mult).then_inc(S("f_ready"), 1)
                if n - 1 in col_at:
                    m = col_at[n - 1]
                    dve.wait_ge(S("col_mul"), m + 1)
                    if m >= 2:
                        dve.wait_ge(S("col_used"), m - 1)
                    dve.tensor_reduce(cols[:, m % 2, :], colw[:, m % 2, :, :].rearrange("p k c -> p c k"), AX_X,
                                      ALU.add).then_inc(S("col_sum"), 1)
                if s.kind == "wo" and s.j == 3:
                    x_norm(1)
                if s.kind == "dn" and s.j == 3 and s.last:
                    x_norm(2)
                    x_norm(3)
                if s.kind == "fv" and s.j == 1:
                    for m in range(12, 21):
                        attn_tick(m)
                if s.kind == "o2" and s.j == 3:
                    x_norm(4)


_INS = ["x", "c", "w_ada", "b_ada", "ln1", "ln2", "w_in", "conv_w", "ssm_conv_w", "ssm_conv_b", "dt_bias", "a_log",
        "d_skip", "ssm_norm_w", "w_conv_out", "w_ssm_out", "w_o", "w_up", "w_down", "final_norm", "c_2", "ln1_g_2",
        "ln2_g_2", "w_ada_2", "b_ada_2", "w_in_2", "b_f_2", "fox_qk_g_2", "diff_qk_g_2", "diff_lam_2", "diff_norm_g_2",
        "w_out_2", "w_gate_2", "w_up_2", "w_down_2"]


def kernel(**inputs):
    import numpy as _np
    import concourse.bacc as _bacc
    from concourse import mybir as _mybir
    from concourse.bass_utils import run_bass_kernel_spmd as _run

    nc = _bacc.Bacc("TRN2", target_bir_lowering=False, num_devices=1)
    arrays, args = {}, {}
    for name in _INS:
        x = _np.ascontiguousarray(inputs[name])
        arrays[f"in_{name}"] = x
        args[name] = nc.dram_tensor(f"in_{name}", x.shape, _mybir.dt.from_np(x.dtype), kind="ExternalInput").ap()
    out = nc.dram_tensor("out", (1, T, D), F32, kind="ExternalOutput").ap()
    build(nc, args, out)
    r = _run(nc, [arrays], core_ids=[0])
    return r.results[0]["out"]
```

```python
from contextlib import ExitStack

import numpy as np
import concourse.bass as bass
from concourse import mybir

F32 = mybir.dt.float32
F32R = mybir.dt.float32r
I32 = mybir.dt.int32
ALU = mybir.AluOpType
ACT = mybir.ActivationFunctionType
AX_X = mybir.AxisListType.X

P = 128
T = 256
TT = T // P
D = 1024
KB = D // P
CW = 256
NB = CW // P
DSSM = 2 * D
HEADS = 32
GROUPS = 8
HD = 64
DFF1 = 4 * D
DFF2 = 2816
EPS = 1e-6
NEG = -1.0e30
LAM_INIT = 0.2
NRAW, NHL, NACC, NF = 3, 3, 3, 4

U1, YC, YS, MG, U2, HID, U3, MX, U4, HID2 = 0, 8, 16, 32, 40, 48, 80, 88, 96, 104


class Step:

    def __init__(self, kind, j, src, kts, cols, act, kt0=0, k=0, nk=1):
        self.kind, self.j, self.src, self.kts, self.cols = kind, j, src, kts, cols
        self.act, self.kt0, self.k, self.nk = act, kt0, k, nk
        self.tokens_out = kind in ("dt", "fv", "dv", "fg")
        self.last = k == nk - 1
        self.g = None


def plan(a):
    steps = []

    def add(kind, j, w, r0, rows, c0, cols, act, kt0=0, k=0, nk=1):
        steps.append(Step(kind, j, w[r0:r0 + rows, c0:c0 + cols], rows // P, cols, act, kt0, k, nk))

    w_in = a["w_in"][0]
    GL, CB, CC, CX, Z, XBC = 0, 2 * D, 3 * D, 4 * D, 5 * D, 5 * D + DSSM
    DT = XBC + DSSM + 2 * GROUPS * P
    add("dt", 0, w_in, 0, D, DT, HEADS, U1)
    for j in range(16):
        add("xbc", j, w_in, 0, D, XBC + (2 * j + 16) % 32 * P, CW, U1)
    for j in range(4):
        add("cc", j, w_in, 0, D, CC + j * CW, CW, U1)
        add("cx", j, w_in, 0, D, CX + j * CW, CW, U1)
        add("cb", j, w_in, 0, D, CB + j * CW, CW, U1)
    for j in range(4):
        add("gc", j, w_in, 0, D, GL + j * CW, CW, U1)
        add("co", j, a["w_conv_out"][0], 0, D, j * CW, CW, YC)
    for j in range(8):
        add("z", j, w_in, 0, D, Z + j * CW, CW, U1)
    for j in range(4):
        add("gs", j, w_in, 0, D, GL + D + j * CW, CW, U1)
        for k in range(2):
            add("so", j, a["w_ssm_out"][0], k * D, D, j * CW, CW, YS, k * KB, k, 2)
    for j in range(4):
        add("wo", j, a["w_o"][0], 0, D, j * CW, CW, MG)
    for j in range(DFF1 // CW):
        add("up", j, a["w_up"][0], 0, D, j * CW, CW, U2)
    for j in range(4):
        for k in range(4):
            add("dn", j, a["w_down"][0], k * D, D, j * CW, CW, HID, k * KB, k, 4)
    w2 = a["w_in_2"][0]
    for kind, j, c0 in (("dq", 0, 1544), ("dk", 0, 2056), ("dv", 0, 2568), ("fg", 0, 1536),
                        ("dq", 1, 1800), ("dk", 1, 2312), ("dv", 1, 2824),
                        ("fq", 0, 0), ("fk", 0, 512), ("fq", 1, 256), ("fk", 1, 768), ("fv", 0, 1024), ("fv", 1, 1280)):
        add(kind, j, w2, 0, D, c0, 8 if kind == "fg" else CW, U3)
    for j in range(4):
        add("o2", j, a["w_out_2"][0], 0, D, j * CW, CW, MX)
    for j in range(DFF2 // CW):
        add("gt", j, a["w_gate_2"][0], 0, D, j * CW, CW, U4)
        add("u2", j, a["w_up_2"][0], 0, D, j * CW, CW, U4)
    for j in range(4):
        for k, rows in enumerate((D, D, DFF2 - 2 * D)):
            add("d2", j, a["w_down_2"][0], k * D, rows, j * CW, CW, HID2, k * KB, k, 3)
    g = 0
    for s in steps:
        if s.k == 0:
            s.g = g
            g += NB
        else:
            s.g = prev.g
        prev = s
    return steps


def build(nc, a, out):
    steps = plan(a)
    NS = len(steps)
    first = {}
    for n, s in enumerate(steps):
        first.setdefault((s.kind, s.j, s.k), n)
    start_of = {}
    for n, s in enumerate(steps):
        start_of.setdefault(s.kind, n)
    QK_ORDER = [(s.kind, s.j) for s in steps if s.kind in ("dq", "dk", "fq", "fk")]
    X0, C0, Z0, I0 = (start_of[k] for k in ("xbc", "cc", "z", "dq"))
    SCAN0 = C0 + 1
    NA0 = 2 * D // CW
    NCOL = 12 * KB - NB * NA0
    XCOL = 2 * KB
    ACOL = NCOL - KB
    col_step = [1 + m if m < XCOL else SCAN0 + 17 + m - XCOL if m < ACOL else start_of["o2"] + 2 + m - ACOL
                for m in range(NCOL)]
    col_at = {n: m for m, n in enumerate(col_step)}
    MOD1_AT, MOD2_AT, MOD3_AT, MOD4_AT = (col_step[c - NB * NA0 - 1] + 3 for c in (48, 64, 88, 96))
    tick_at = {(I0 + slot // NB, slot % NB): m
               for m, slot in enumerate((6, 7, 9, 10, 14, 15, 16, 18, 20, 21, 22, 23, 24, 25))}
    LO_NB = 1
    last_ticks = range(len(tick_at), 21)

    stream = [("ada", n) for n in range(NA0)] + [("step", 0), ("step", 1)]
    for n in range(2, NS):
        stream.append(("step", n))
        if n - 4 in col_at:
            stream.append(("col", col_at[n - 4]))
    raw_stream = [item for item in stream if item[0] != "col"]
    raw_at = {item: r for r, item in enumerate(raw_stream)}

    with ExitStack() as ctx, ExitStack() as programs:
        def sb(name, shape, dt=F32, stack=ctx):
            return stack.enter_context(nc.sbuf_tensor(name, shape, dt))

        sems = {}

        class Sems:
            def __call__(self, name):
                if name not in sems:
                    sems[name] = ctx.enter_context(nc.semaphore(name))
                return sems[name]

        S = Sems()

        raw = sb("raw", [P, NRAW, KB, CW])
        w_hi = sb("w_hi", [P, NHL, KB, CW], F32R)
        w_lo = sb("w_lo", [P, NHL, KB, CW], F32R)
        xT = sb("xT", [P, KB, T])
        uh = sb("uh", [P, KB, T], F32R)
        ul = sb("ul", [P, KB, T], F32R)
        par = sb("par", [P, 3, P])
        cact = sb("cact", [P, 16])
        mod = sb("mod", [P, 96])
        gain = sb("gain", [P, 5, KB])
        small = sb("small", [P, 16])
        ident = sb("ident", [P, P])
        ones = sb("ones", [P, P])
        blk64 = sb("blk64", [P, P])
        tri = sb("tri", [P, T])
        min_st = sb("min_st", [P, T])
        mask_ts = sb("mask_ts", [P, 3 * P])
        dist_ts = sb("dist_ts", [P, 3 * P])
        eps = sb("eps", [P, 1])
        fr = sb("fr", [P, NF, T])
        stg = sb("stg", [P, 2, T + 3])
        cv = sb("cv", [P, 2, T])
        cct = sb("cct", [P, 2, T])
        gt = sb("gt", [P, 2, T])
        sq = sb("sq", [P, 4, T])
        rt = sb("rt", [P, 2, T])
        diag_a = sb("diag_a", [P, 2, 2 * P])
        diag_b = stg[:, :, :].rearrange("p a b -> p (a b)")[:, 0:4 * P].rearrange("p (a b) -> p a b", b=2 * P)
        DIAG = [diag_a[:, 0, :], diag_a[:, 1, :], diag_b[:, 0, :], diag_b[:, 1, :]]
        maps = sb("maps", [P, 3 * 2 * 3 * P])
        seg, ex, sc = (maps[:, i * 6 * P:(i + 1) * 6 * P].rearrange("p (a b) -> p a b", b=3 * P) for i in range(3))
        colw = maps[:, 0:2 * KB * P].rearrange("p (s k c) -> p s k c", s=2, c=P)
        cols = maps[:, 2 * KB * P:(2 * KB + 2) * P].rearrange("p (s c) -> p s c", c=P)
        nmx = sb("nmx", [P, 2, 2])
        qs = sb("qs", [P, 8])
        qr = sb("qr", [P, 8])
        qt = sb("qt", [P, 8])
        zr = sb("zr", [P, GROUPS, TT])
        rs = sb("rs", [P, 4, 2])
        rr = sb("rr", [P, 4, 2])
        EX = [ex[:, 0, :], ex[:, 1, :]] + [t_[:, :, :].rearrange("p a b -> p (a b)")[:, 0:3 * P] for t_ in (gt, cct)]
        dtr = cct[:, :, :].rearrange("p a b -> p (a b)")[:, 0:6 * TT * HEADS]\
            .rearrange("p (a b) -> p a b", b=TT * HEADS)
        dt_sb = sb("dt_sb", [P, TT, HEADS])
        dta = sb("dta", [P, TT, HEADS])
        nac = sb("nac", [P, TT, HEADS])
        hb = sb("hb", [P, 3, HEADS])
        nega = sb("nega", [P, HEADS])
        dsk = sb("dsk", [P, HEADS // 2])
        bf = sb("bf", [P, 8])
        lamw = gt[:, 0, :].rearrange("p (a b) -> p a b", b=HD)
        nlf = sb("nlf", [P, TT, 8])
        fcum = sb("fcum", [P, TT, 8])

        arena = ExitStack()
        xs = sb("xs", [P, 16, T], F32, arena)
        bct = sb("bct", [P, 16, T], F32, arena)
        ada_sum = bct[:, 0:2, :]
        xdt = sb("xdt", [P, TT, DSSM], F32, arena)
        ych = sb("ych", [P, KB, T], F32R, arena)
        ycl = sb("ycl", [P, KB, T], F32R, arena)
        mc = sb("mc", [P, KB, T], F32, arena)
        arena.close()
        arena = ExitStack()
        sb("skip_xs", [P, 16, T], F32, arena)
        ysh = sb("ysh", [P, 16, T], F32R, arena)
        ysl = sb("ysl", [P, 16, T], F32R, arena)
        arena.close()
        arena = ExitStack()
        hidh = sb("hidh", [P, 32, T], F32R, arena)
        hidl = sb("hidl", [P, 32, T], F32R, arena)
        outb = sb("outb", [P, TT, D], F32, arena)
        arena.close()
        arena = ExitStack()
        qk = sb("qk", [P, 16, T], F32, arena)
        v = sb("v", [P, TT, D], F32, arena)
        mxh = sb("mxh", [P, KB, T], F32R, arena)
        mxl = sb("mxl", [P, KB, T], F32R, arena)
        arena.close()
        sb("arena", [P, 18, D])

        acc = [ctx.enter_context(nc.psum_tensor(f"acc{i}", [P, 512], F32)) for i in range(NACC)]
        M0, M1, M2, M3, M4 = (ctx.enter_context(nc.psum_tensor(f"m{i}", [P, 512], F32)) for i in range(5))

        c_cols, ln_cols, ada_b = par[:, 0, 0:16], par[:, 0, 16:32], par[:, 0, 32:128]
        conv_w, norm_w, final_w = par[:, 1, 0:24], par[:, 1, 24:40], par[:, 1, 40:48]
        ln2_cols, ssm_b, qk_gain, dn_gain = par[:, 1, 48:64], par[:, 1, 64:96], par[:, 1, 96:100], par[:, 1, 100:101]
        ssm_w = par[:, 2, :]
        SH = [mod[:, 0:8], mod[:, 24:32], None, mod[:, 48:56], mod[:, 72:80]]
        SCL = [mod[:, 8:16], mod[:, 32:40], None, mod[:, 56:64], mod[:, 80:88]]
        GATE = [mod[:, 16:24], mod[:, 40:48], mod[:, 64:72], mod[:, 88:96]]
        LN = [ln_cols[:, 0:8], ln_cols[:, 8:16], None, ln2_cols[:, 0:8], ln2_cols[:, 8:16]]
        NORM_U = [U1, U2, None, U3, U4]
        NEG_LAM = small[:, 0:1]

        def mod_bank(col):
            return M0 if col < NB * NA0 + XCOL else M1 if col < 48 else M2 if col < 64 else M3 if col < 88 else M1

        def dest(i):
            for base, hi, lo, n0 in ((HID2, hidh, hidl, 0), (U4, uh, ul, 0), (MX, mxh, mxl, None), (U3, uh, ul, 0),
                                     (HID, hidh, hidl, 0), (U2, uh, ul, 0), (MG, ych, ycl, 0), (YS, ysh, ysl, 0),
                                     (YC, ych, ycl, 0), (U1, uh, ul, 0)):
                if i >= base:
                    b = i - base
                    if n0 is None:
                        b = (b + 4) % 8
                    return hi[:, b, :], lo[:, b, :]

        def operands(base):
            return {U1: (uh, ul), YC: (ych, ycl), YS: (ysh, ysl), MG: (ych, ycl), U2: (uh, ul), HID: (hidh, hidl),
                    U3: (uh, ul), MX: (mxh, mxl), U4: (uh, ul), HID2: (hidh, hidl)}[base]

        def raw_of(item, s=None):
            slot = raw_at[item] % NRAW
            return raw[:, slot, 0:s.kts, 0:s.cols] if s else raw[:, slot, :, :]

        def wait_raw(eng, item):
            r = raw_at[item]
            eng.wait_ge(S(f"raw_in{r % NRAW}"), 16 * (r // NRAW + 1))

        rows = seg[:, :, :].rearrange("p a (b c) -> p (a b) c", c=P)
        N_PAR, N_VEC = 18, 5
        N_CONST = 20

        def drained(s, nb):
            i = NB * s.j + nb
            if s.kind in ("dq", "dk", "fq", "fk"):
                return "qk_raw", NB * QK_ORDER.index((s.kind, s.j)) + nb + 1
            return {
                "dt": ("dt_z", nb + 1), "fg": ("fg_z", nb + 1), "xbc": ("cv_init", i + 1), "cc": ("cc_out", i + 1),
                "cx": ("cx_in", i + 1), "cb": ("f_ready", YC + i + 1), "gc": ("gate", i + 1), "gs": ("gate", 9 + i),
                "co": ("gate_used", i + 1), "so": ("gate_used", 9 + i), "z": ("sz_done", i + 1),
                "wo": ("x_ready", KB + i + 1), "dn": ("x_ready", 2 * KB + i + 1), "o2": ("x_ready", 4 * KB + i + 1),
                "d2": ("x_ready", 5 * KB + i + 1), "up": ("relu", i + 1), "gt": ("silu_g", i + 1),
                "u2": ("f_ready", HID2 + i + 1), "dv": ("v_out", i + 1), "fv": ("v_out", 5 + i),
            }[s.kind]

        def product_with(w):
            return w // 2 if w < 8 else w - 4

        def product_of(w):
            return product_with(w) if 0 <= w < 16 and (w >= 8 or w % 2) else None

        def split_late(n):
            return I0 <= n < start_of["o2"]

        def z_blocks(zs):
            return range(NB * (zs - 5), NB * (zs - 4)) if 5 <= zs < 9 else range(8, 16) if zs == 9 else ()

        unfinished = [0]
        for s_ in steps:
            unfinished.append(unfinished[-1] + (not s_.last))

        def wait_step(eng, n):
            if steps[n].last:
                eng.wait_ge(S("acc_ready"), steps[n].g + NB)
            else:
                eng.wait_ge(S("part_done"), unfinished[n + 1])

        def row_loads():
            st = rows
            def vec(name, n):
                ap = a[name]
                return ap[0].rearrange("(b f) -> b f", f=P) if len(ap.shape) == 2 else ap.rearrange("(b f) -> b f", f=P)
            return [
                (st[0:8, 0, :], vec("c", 8)), (st[8:16, 0, :], vec("c_2", 8)),
                (st[16:24, 0, :], vec("ln1", 8)), (st[24:32, 0, :], vec("ln2", 8)),
                (st[32:80, 0, :], vec("b_ada", 48)), (st[80:128, 0, :], vec("b_ada_2", 48)),
                (st[0:24, 1, :], a["conv_w"][0].rearrange("k (b f) -> (k b) f", f=P)),
                (st[24:40, 1, :], vec("ssm_norm_w", 16)), (st[40:48, 1, :], vec("final_norm", 8)),
                (st[48:56, 1, :], vec("ln1_g_2", 8)), (st[56:64, 1, :], vec("ln2_g_2", 8)),
                (st[64:96, 1, :], vec("ssm_conv_b", 32)),
                (st[96:98, 1, 0:HD], a["fox_qk_g_2"][0]), (st[96:98, 1, HD:P], a["fox_qk_g_2"][0]),
                (st[98:100, 1, 0:HD], a["diff_qk_g_2"][0]), (st[98:100, 1, HD:P], a["diff_qk_g_2"][0]),
                (st[100:101, 1, :], a["diff_norm_g_2"]),
                (st[:, 2, :], a["ssm_conv_w"][0].rearrange("k (b f) -> (k b) f", f=P)),
            ]

        def row_vectors():
            return [(hb[:, 0, :], a["dt_bias"].to_broadcast([P, HEADS])), (hb[:, 1, :], a["a_log"].to_broadcast([P, HEADS])),
                    (hb[:, 2, :], a["d_skip"].to_broadcast([P, HEADS])), (bf[:, :], a["b_f_2"].to_broadcast([P, 8])),
                    (lamw[:, :, :].rearrange("p a b -> p (a b)"),
                     a["diff_lam_2"].rearrange("o a b -> o (a b)").to_broadcast([P, 4 * HD]))]

        block = programs.enter_context(nc.Block())

        @block.sync
        def _(sp):
            x_tok = xdt[:, :, 0:D]
            sp.dma_start(x_tok, a["x"][0].rearrange("(a p) d -> p a d", p=P)).then_inc(S("x_in"), 16)
            for item in stream:
                kind, n = item
                if kind == "col":
                    if n == 0:
                        sp.wait_ge(S("par_done"), 1)
                    elif n == XCOL:
                        sp.wait_ge(S("y_done"), HEADS)
                    elif n == ACOL:
                        sp.wait_ge(S("pv_done"), 12)
                    if n >= 2:
                        sp.wait_ge(S("col_sum"), n - 1)
                    w, c = (a["w_ada"][0], n + NB * NA0) if n + NB * NA0 < 48 else (a["w_ada_2"][0], n + NB * NA0 - 48)
                    sp.dma_start(colw[:, n % 2, :, :], w[:, c * P:(c + 1) * P].rearrange("(k p) n -> p k n", p=P))\
                      .then_inc(S(f"col_in{n % 2}"), 16)
                    continue
                r = raw_at[item]
                if r >= NRAW:
                    before, b = raw_stream[r - NRAW]
                    if before == "step":
                        sp.wait_ge(S("lo_ready"), b + 1)
                    else:
                        sp.wait_ge(S("ada_sum"), b + 1)
                if kind == "step":
                    s = steps[n]
                    dst, src = raw_of(item, s), s.src
                else:
                    dst, src = raw_of(item), a["w_ada"][0][:, n * CW:(n + 1) * CW]
                sp.dma_start(dst, src.rearrange("(k p) n -> p k n", p=P)).then_inc(S(f"raw_in{r % NRAW}"), 16)
            for b in range(KB):
                sp.wait_ge(S("out_ready"), b + 1)
                sp.dma_start(out[0].rearrange("(a p) d -> p a d", p=P)[:, :, b * P:(b + 1) * P],
                             outb[:, :, b * P:(b + 1) * P]).then_inc(S("out_done"), 16)
            sp.wait_ge(S("out_done"), 16 * KB)

        @block.gpsimd
        def _(pool):
            pool.memset(rows[:, 0:3, :], 0.0).then_inc(S("par_zero"), 1)
            pool.memset(ident[:, :], 0.0).then_inc(S("pc"), 1)
            pool.memset(ones[:, :], 1.0).then_inc(S("pc"), 1)
            pool.memset(blk64[:, :], 0.0).then_inc(S("pc"), 1)
            pool.memset(tri[:, :], 1.0).then_inc(S("pc"), 1)
            pool.memset(min_st[:, :], 0.0).then_inc(S("pc"), 1)
            pool.memset(mask_ts[:, :], 0.0).then_inc(S("pc"), 1)
            pool.memset(eps[:, :], EPS).then_inc(S("pc"), 1)
            pool.memset(stg[:, :, 0:3], 0.0).then_inc(S("pc"), 1)
            distf = ex[:, 0, :]
            disti = ex[:, 1, :].bitcast(I32)
            pool.iota(disti[:, 0:P], pattern=[[1, P]], base=0, channel_multiplier=-1).then_inc(S("pc"), 1)
            pool.iota(disti[:, P:3 * P], pattern=[[1, T]], base=-P, channel_multiplier=-1).then_inc(S("pc"), 1)
            pool.wait_ge(S("pc"), 10)
            pool.affine_select(out=ident[:, :], in_=ident[:, :], compare_op=ALU.not_equal, fill=1.0, base=0,
                               pattern=[[-1, P]], channel_multiplier=1).then_inc(S("pc"), 1)
            for i, o in enumerate((0, HD)):
                pool.wait_ge(S("pc"), 11 + i)
                pool.memset(blk64[o:o + HD, o:o + HD], 1.0).then_inc(S("pc"), 1)
            pool.wait_ge(S("pc"), 13)
            pool.affine_select(out=tri[:, :], in_=tri[:, :], compare_op=ALU.is_ge, fill=0.0, base=0,
                               pattern=[[1, T]], channel_multiplier=-1).then_inc(S("pc"), 1)
            pool.affine_select(out=min_st[:, :], in_=min_st[:, :], compare_op=ALU.is_ge, fill=NEG, base=0,
                               pattern=[[1, T]], channel_multiplier=-1).then_inc(S("pc"), 1)
            pool.tensor_copy(distf, disti).then_inc(S("pc"), 1)
            pool.wait_ge(S("pc"), 16)
            for dst, src in ((mask_ts, mask_ts[:, :]), (dist_ts, distf)):
                pool.affine_select(out=dst[:, 0:P], in_=src[:, 0:P], compare_op=ALU.is_ge, fill=NEG, base=0,
                                   pattern=[[-1, P]], channel_multiplier=1).then_inc(S("pc"), 1)
                pool.affine_select(out=dst[:, P:3 * P], in_=src[:, P:3 * P], compare_op=ALU.is_ge, fill=NEG, base=P,
                                   pattern=[[-1, T]], channel_multiplier=1).then_inc(S("pc"), 1)

            def lo_part(i):
                hi, lo = dest(i)
                pool.wait_ge(S("act_hi"), i + 1)
                pool.tensor_tensor(lo, fr[:, i % NF, :], hi.bitcast(F32), ALU.subtract).then_inc(S("act_lo"), 1)

            def attn_tick(m):
                w = m - 1
                if w < 16:
                    pool.wait_ge(S("rr_ready"), w + 1)
                    if w >= 4:
                        pool.wait_ge(S("tr_done"), product_with(w - 4) + 1)
                    for t in range(TT):
                        ins = pool.tensor_scalar(DIAG[w % 4][:, t * P:(t + 1) * P], ident[:, :], rr[:, w % 4, t:t + 1],
                                                 None, ALU.mult)
                    ins.then_inc(S("diag_done"), 1)
                c = product_of(m - 5)
                if c is not None and c >= 4 and c % 2:
                    lo_part(MX + 4 + (c - 4) // 2)
                c = product_of(m - 6)
                if c is not None and c < 4:
                    lo_part(MX + c)

            for n in range(NA0):
                if n == 0:
                    pool.wait_ge(S("cact"), 1)
                wait_raw(pool, ("ada", n))
                w = raw_of(("ada", n))[:, KB // 2:KB, :]
                pool.tensor_tensor(w, w, cact[:, KB // 2:KB].unsqueeze(2).to_broadcast([P, KB // 2, CW]), ALU.mult)\
                    .then_inc(S("ada_mul_b"), 1)
            for i in range(U1, YC):
                lo_part(i)
            for n in range(NS):
                s = steps[n]
                for nb in range(NB):
                    if (n, nb) in tick_at and tick_at[n, nb]:
                        attn_tick(tick_at[n, nb])
                    if s.kind == "cb":
                        lo_part(YC + NB * s.j + nb)
                    q = NB * (n - SCAN0) + nb
                    if 0 <= q < HEADS:
                        pool.wait_ge(S("exp_done"), q + 1)
                        pool.wait_ge(S("sc_done"), q // 4 + 1)
                        pool.tensor_tensor(ex[:, q % 2, :], ex[:, q % 2, :], sc[:, q // 4 % 2, :],
                                           ALU.mult).then_inc(S("mul_done"), 1)
                zs = n - Z0
                if 0 <= zs < 8:
                    for nb in range(NB):
                        b = NB * zs + nb
                        pool.wait_ge(S("sz_done"), b + 1)
                        pool.wait_ge(S("yadd_done"), b + 1)
                        pool.tensor_tensor(xs[:, b, :], xs[:, b, :], gt[:, nb, :], ALU.mult).then_inc(S("yz_done"), 1)
                for b in z_blocks(zs):
                    lo_part(YS + b)
                if s.kind == "so" and s.last:
                    for nb in range(NB):
                        lo_part(MG + NB * s.j + nb)
                if s.kind == "up" and s.j == 0:
                    for i in range(U2, HID):
                        lo_part(i)
                if s.kind == "up":
                    for nb in range(NB):
                        lo_part(HID + NB * s.j + nb)
                if s.kind == "dq" and s.j == 0:
                    for i in range(U3, MX):
                        lo_part(i)
                if s.kind == "fv" and s.j == 1:
                    for m in last_ticks:
                        attn_tick(m)
                if s.kind == "gt" and s.j == 0:
                    for i in range(U4, HID2):
                        lo_part(i)
                if s.kind == "u2":
                    for nb in range(NB):
                        lo_part(HID2 + NB * s.j + nb)
                if n in col_at:
                    m = col_at[n]
                    cc = 8 * (m + NB * NA0 >= 48)
                    pool.wait_ge(S("cact"), 1)
                    pool.wait_ge(S(f"col_in{m % 2}"), 16 * (m // 2 + 1))
                    pool.tensor_tensor(colw[:, m % 2, :, :], colw[:, m % 2, :, :],
                                       cact[:, cc:cc + KB].unsqueeze(2).to_broadcast([P, KB, P]), ALU.mult)\
                        .then_inc(S("col_mul"), 1)

        @block.scalar
        def _(act):
            def split_hi(n):
                s = steps[n]
                wait_raw(act, ("step", n))
                if n >= NHL:
                    wait_step(act, n - NHL)
                act.activation(w_hi[:, n % NHL, 0:s.kts, 0:s.cols], raw_of(("step", n), s), ACT.Copy)\
                   .then_inc(S("hi_ready"), 1)

            def hi_part(i, shift=None):
                hi, _ = dest(i)
                x = fr[:, i % NF, :]
                act.wait_ge(S("f_ready"), i + 1)
                if shift is None:
                    act.activation(hi, x, ACT.Copy).then_inc(S("act_hi"), 1)
                else:
                    act.activation(hi, x, ACT.Identity, bias=shift)
                    act.activation(x, x, ACT.Identity, bias=shift).then_inc(S("act_hi"), 1)

            def x_square(i):
                act.wait_ge(S("x_ready"), i + 1)
                if i >= 4:
                    act.wait_ge(S("xsum_done"), i - 3)
                act.activation(sq[:, i % 4, :], xT[:, i % KB, :], ACT.Square).then_inc(S("xsq"), 1)

            def log_exp_table():
                act.preload_act_table_set("natural_log_exp_and_others")

            def inverse_root(dst, sums, n, done):
                link(act.activation(dst, sums, ACT.Ln, bias=eps[:, :], scale=1.0 / n))
                act.activation(dst, dst, ACT.Exp, scale=-0.5).then_inc(S(done), 1)

            def x_root(n):
                log_exp_table()
                act.wait_ge(S("xsum_done"), KB * (n + 1))
                inverse_root(rt[:, 0, :], M4[:, 0:T], D, "xroot")

            def early_ada(m):
                if m == 0:
                    act.wait_ge(S("cact"), 1)
                wait_raw(act, ("ada", m))
                for k in range(KB // 2):
                    w = raw_of(("ada", m))[:, k, :]
                    ins = act.activation(w, w, ACT.Identity, scale=cact[:, k:k + 1])
                ins.then_inc(S("ada_mul_a"), 1)

            def x_norm(n):
                if n:
                    x_root(n)
                if NORM_U[n] is not None:
                    for b in range(KB):
                        hi_part(NORM_U[n] + b, SH[n][:, b:b + 1] if b % 2 == 0 else None)

            chain = [0]

            def link(ins):
                chain[0] += 1
                ins.then_inc(S("act_chain"), 1)
                act.wait_ge(S("act_chain"), chain[0])

            def log1p_exp_parts(w, z, k):
                act.wait_ge(S(("dt_z", "fg_z")[k]), NB)
                link(act.activation(w[:, 0, :], z, ACT.Abs))
                act.activation(w[:, 1, :], w[:, 0, :], ACT.Exp, scale=-1.0).then_inc(S("sp_e"), 1)
                act.wait_ge(S("sp_w"), k + 1)
                act.activation(w[:, 3, :], w[:, 2, :], ACT.Ln).then_inc(S("sp_ln"), 1)

            act.wait_ge(S("par_zero"), 1)
            for dst, src in row_loads():
                act.dma_start(dst, src).then_inc(S("par_in"), 16)
            for dst, src in row_vectors():
                act.dma_start(dst, src).then_inc(S("vec_in"), 16)
            act.wait_ge(S("pc"), N_CONST)
            act.wait_ge(S("par_done"), 1)
            act.activation(cact[:, :], c_cols, ACT.Silu).then_inc(S("cact"), 1)
            log_exp_table()
            early_ada(0)
            early_ada(1)
            early_ada(2)
            for i in range(KB):
                x_square(i)
            x_root(0)
            act.wait_ge(S("vec_in"), 16 * N_VEC)
            act.activation(nega[:, :], hb[:, 1, :], ACT.Exp).then_inc(S("nega"), 1)
            act.wait_ge(S("lam_dots"), 1)
            act.activation(small[:, 4:6], small[:, 2:4], ACT.Exp).then_inc(S("lam_exp"), 1)
            for m in range(3, NA0):
                early_ada(m)
            split_hi(0)
            x_norm(0)
            split_hi(1)

            def attn_tick(m):
                if m < 16:
                    b, e = m % 2, EX[m % 4]
                    act.wait_ge(S("mx_done"), m + 1)
                    if m == 0:
                        act.wait_ge(S("col_used"), ACOL)
                    if m >= 4:
                        act.wait_ge(S("tr_done"), product_with(m - 4) + 1)
                    act.activation(e[:, 0:P], seg[:, b, 0:P], ACT.Exp, bias=nmx[:, b, 0:1],
                                   accum_out=rs[:, m % 4, 0:1])
                    act.activation(e[:, P:3 * P], seg[:, b, P:3 * P], ACT.Exp, bias=nmx[:, b, 1:2],
                                   accum_out=rs[:, m % 4, 1:2]).then_inc(S("ex_done"), 1)
                c = product_of(m - 2)
                if c is not None:
                    act.wait_ge(S("tr_done"), c + 1)
                    if c >= 2:
                        act.wait_ge(S("pv_done"), c - 1)
                    act.activation(sc[:, c % 2, :], M3[:, 0:3 * P], ACT.Copy).then_inc(S("pt_done"), 1)
                c = product_of(m - 4)
                if c is not None and c < 4:
                    act.wait_ge(S("o_copied"), c + 1)
                    act.activation(sq[:, 0, :], cv[:, c % 2, :], ACT.Square).then_inc(S("osq"), 1)
                c = product_of(m - 5)
                if c is not None and c < 4:
                    act.wait_ge(S("osum"), c + 1)
                    if c:
                        act.wait_ge(S("f_ready"), MX + c)
                    inverse_root(sq[:, 1, :], M0[:, 0:T], P, "oroot")
                if c is not None and c >= 4 and c % 2:
                    hi_part(MX + 4 + (c - 4) // 2)
                c = product_of(m - 6)
                if c is not None and c < 4:
                    hi_part(MX + c)

            def out_copy(b):
                act.wait_ge(S("otr_done"), b + 1)
                act.activation(outb[:, :, b * P:(b + 1) * P], (M3, M4)[b % 2][:, 0:T].rearrange("p (a c) -> p a c", c=P),
                               ACT.Copy).then_inc(S("out_ready"), 1)

            jq = 0
            pending = []
            for n in range(NS):
                s = steps[n]
                if n + 2 < NS and not split_late(n):
                    split_hi(n + 2)
                zs = n - Z0
                if 1 <= zs < 9:
                    for nb in range(NB):
                        act.wait_ge(S("yz_done"), NB * (zs - 1) + nb + 1)
                        if zs >= 3:
                            act.wait_ge(S("zsum_done"), zs - 2)
                        act.activation(sq[:, 2 * (zs % 2) + nb, :], xs[:, NB * (zs - 1) + nb, :],
                                       ACT.Square).then_inc(S("zsq"), 1)
                if zs in (5, 9):
                    log_exp_table()
                    g = zs - 5
                    act.wait_ge(S("zsum_done"), g + 4)
                    inverse_root(zr[:, g:g + 4, :], M3[:, 2 * g:2 * g + 8].rearrange("p (a b) -> p a b", b=TT), 2 * P,
                                 "zroot")
                for nb in range(NB):
                    bank = acc[(s.g + nb) % NACC]
                    ps, free = bank[:, 0:T], S(drained(s, nb)[0])
                    takes = s.last and s.kind in ("xbc", "cc", "gc", "z", "gs", "up", "dq", "dk", "fq", "fk", "fv",
                                                  "dv", "gt")
                    if takes:
                        act.wait_ge(S("acc_ready"), s.g + nb + 1)
                    elif pending:
                        hi_part(pending.pop())
                    if s.kind == "xbc":
                        i = NB * s.j + nb
                        fb = (i + 16) % 32
                        if i >= 2:
                            act.wait_ge(S("conv_done"), i - 1)
                            act.wait_ge(S("silu_done"), i - 1)
                        act.activation(stg[:, i % 2, 3:T + 3], ps, ACT.Copy).then_inc(S("stg_ready"), 1)
                        act.activation(cv[:, i % 2, :], ps, ACT.Identity, bias=ssm_b[:, fb:fb + 1],
                                       scale=ssm_w[:, 96 + fb:97 + fb]).then_inc(free, 1)
                    if s.kind == "cc":
                        if s.j:
                            act.wait_ge(S("cx_in"), NB * (s.j - 1) + nb + 1)
                        act.activation(cct[:, nb, :], ps, ACT.Copy).then_inc(free, 1)
                    if s.kind in ("gc", "gs"):
                        c = (4 * (s.kind == "gs") + s.j) * NB + nb
                        if c >= NB:
                            act.wait_ge(S("gate_used"), c - NB + 1)
                        if c >= 8:
                            act.wait_ge(S("yz_done"), 16)
                        act.activation(gt[:, nb, :], ps, ACT.Sigmoid).then_inc(free, 1)
                    if s.kind == "z":
                        i = NB * s.j + nb
                        if i >= 2:
                            act.wait_ge(S("yz_done"), i - 1)
                        else:
                            act.wait_ge(S("gate_used"), 8)
                        act.activation(gt[:, nb, :], ps, ACT.Silu).then_inc(free, 1)
                    if s.kind == "up":
                        i = NB * s.j + nb
                        if i >= 2:
                            act.wait_ge(S("f_ready"), HID + i - 1)
                        act.activation(gt[:, nb, :], ps, ACT.Relu).then_inc(free, 1)
                    if s.kind == "gt":
                        i = NB * s.j + nb
                        if i >= 2:
                            act.wait_ge(S("f_ready"), HID2 + i - 1)
                        act.activation(gt[:, nb, :], ps, ACT.Silu).then_inc(free, 1)
                    if s.kind in ("dq", "dk", "fq", "fk"):
                        b = {"dq": 0, "dk": 4, "fq": 8, "fk": 12}[s.kind] + NB * s.j + nb
                        if nb == 0 and QK_ORDER.index((s.kind, s.j)):
                            act.wait_ge(S("qsum_done"), QK_ORDER.index((s.kind, s.j)))
                        act.activation(sq[:, 2 + nb, :], ps, ACT.Square).then_inc(S("qsq"), 1)
                        act.activation(qk[:, b, :], ps, ACT.Copy).then_inc(free, 1)
                    if s.kind == "d2" and s.k == 0 and s.j:
                        out_copy(NB * (s.j - 1) + nb)
                    if s.kind in ("fv", "dv"):
                        o = (4 * (s.kind == "dv")) * P + s.j * CW
                        act.activation(v[:, nb, o:o + CW], ps, ACT.Copy).then_inc(free, 1)
                    prev = steps[n - 1].kind if n else ""
                    if nb == 0 and prev in ("dq", "dk", "fq", "fk"):
                        jq += 1
                        act.wait_ge(S("qsum_done"), jq)
                        if jq > 1:
                            act.wait_ge(S("qbc_done"), jq - 1)
                        act.activation(qs[:, :], M0[:, 0:8], ACT.Copy).then_inc(S("qsum_read"), 1)
                        act.wait_ge(S("qsum_read"), jq)
                        inverse_root(qr[:, :], qs[:, :], HD, "qroot")
                    if X0 <= n and NB * (n - X0) + nb - 1 in range(32):
                        i = NB * (n - X0) + nb - 1
                        fb = (i + 16) % 32
                        dst = xs[:, fb, :] if fb < 16 else bct[:, fb - 16, :]
                        act.wait_ge(S("conv_done"), i + 1)
                        act.activation(dst, cv[:, i % 2, :], ACT.Silu).then_inc(S("silu_done"), 1)
                    if takes and pending:
                        hi_part(pending.pop())
                    base = {"cb": YC, "so": MG, "up": HID, "u2": HID2}.get(s.kind)
                    if base is not None and s.last:
                        pending.append(base + NB * s.j + nb)
                    for kind, norm in (("wo", 1), ("dn", 2), ("o2", 4)):
                        if s.kind == kind and s.last:
                            x_square(KB * norm + NB * s.j + nb)
                    q = NB * (n - SCAN0) + nb
                    if 0 <= q < HEADS:
                        if q % 4 == 0:
                            g = q // 4
                            act.wait_ge(S("scores"), g + 1)
                            if g == 0:
                                act.wait_ge(S("col_used"), XCOL)
                            if g >= 2:
                                act.wait_ge(S("mul_done"), 4 * (g - 1))
                            act.activation(sc[:, g % 2, :], M3[:, 0:3 * P], ACT.Copy).then_inc(S("sc_done"), 1)
                        act.wait_ge(S("seg_done"), q + 1)
                        if q >= 2:
                            act.wait_ge(S("y_done"), q - 1)
                        act.activation(ex[:, q % 2, :], seg[:, q % 2, :], ACT.Exp).then_inc(S("exp_done"), 1)
                    if (n, nb) in tick_at:
                        attn_tick(tick_at[n, nb])
                    if split_late(n) and nb == 0:
                        split_hi(n + 2)
                if s.kind == "dt":
                    log1p_exp_parts(dtr[:, 1:6, :], dtr[:, 0, :], 0)
                if s.kind == "fg":
                    log1p_exp_parts(dtr[:, 1:6, 0:16], dtr[:, 0, 0:16], 1)
                for b in z_blocks(zs):
                    hi_part(YS + b)
                if s.kind == "wo" and s.j == 3:
                    x_norm(1)
                if s.kind == "dn" and s.j == 3 and s.last:
                    x_norm(2)
                    for i in range(KB):
                        x_square(3 * KB + i)
                    x_norm(3)
                if s.kind == "fv" and s.j == 1:
                    for m in last_ticks:
                        attn_tick(m)
                if s.kind == "o2" and s.j == 3:
                    x_norm(4)
            out_copy(KB - 2)
            out_copy(KB - 1)


        @block.tensor
        def _(pe):
            free = {}

            def take(bank):
                if bank in free:
                    pe.wait_ge(S(free[bank][0]), free[bank][1])

            pe.wait_ge(S("pc"), N_CONST)
            pe.wait_ge(S("par_in"), 16 * N_PAR)
            for i, bank in enumerate((M1, M2, M3)):
                pe.transpose(bank[:, 0:P], rows[:, i, :], ident[:, :]).then_inc(S("par_t"), 1)
            free["M1"] = free["M2"] = free["M3"] = ("par_done", 1)
            pe.wait_ge(S("x_in"), 16)
            for b in range(KB):
                name, bank = (("M1", M1), ("M2", M2), ("M3", M3))[b % 3]
                take(name)
                for t in range(TT):
                    ins = pe.transpose(bank[:, t * P:(t + 1) * P], xdt[:, t, b * P:(b + 1) * P], ident[:, :])
                ins.then_inc(S("xt_done"), 1)
                free[name] = ("x_ready", b + 1)

            def x_sum(i):
                b = i % KB
                if b == 0:
                    take("M4")
                pe.wait_ge(S("xsq"), i + 1)
                pe.matmul(M4[:, 0:T], ones[:, :], sq[:, i % 4, :], start=(b == 0), stop=(b == KB - 1))\
                  .then_inc(S("xsum_done"), 1)
                if b == KB - 1:
                    free["M4"] = ("xroot", i // KB + 1)

            def ada(n):
                pe.wait_ge(S("ada_sum"), n + 1)
                for nb in range(NB):
                    col = NB * n + nb
                    ins = pe.matmul(M0[:, col:col + 1], ada_sum[:, n % 2, nb * P:(nb + 1) * P], ones[:, 0:1],
                                    start=True, stop=True)
                ins.then_inc(S("ada_used"), 1)

            def ada_column(m):
                col = m + NB * NA0
                if m == 0:
                    pe.wait_ge(S("mod_done"), 1)
                pe.wait_ge(S("col_sum"), m + 1)
                if col == 64:
                    take("M3")
                    free["M3"] = ("mod_done", 5)
                if col == 88:
                    pe.wait_ge(S("l_done"), 16)
                pe.matmul(mod_bank(col)[:, col:col + 1], cols[:, m % 2, :], ones[:, 0:1], start=True, stop=True)\
                  .then_inc(S("col_used"), 1)

            ada(0)
            for i in range(KB):
                x_sum(i)
            for n in range(1, NA0):
                ada(n)

            def product(n, nb):
                s = steps[n]
                g = s.g + nb
                H, L = operands(s.act)
                out_ = acc[g % NACC]
                if nb == 0:
                    pe.wait_ge(S("lo_ready"), n + 1)
                if s.k == 0 and g >= NACC:
                    name, value = drained(*block_of[g - NACC])
                    pe.wait_ge(S(name), value)
                for i, kt in enumerate((4, 5, 6, 7, 0, 1, 2, 3) if s.act == MX else range(s.kts)):
                    need = s.act + s.kt0 + i + 1
                    if need > seen[0]:
                        pe.wait_ge(S("act_lo"), need)
                        seen[0] = need
                    x_hi, x_lo = H[:, s.kt0 + kt, :], L[:, s.kt0 + kt, :]
                    wh, wl = w_hi[:, n % NHL, kt, 0:s.cols], w_lo[:, n % NHL, kt, 0:s.cols]
                    if s.tokens_out:
                        o = out_[:, 0:s.cols]
                        x_hi, x_lo = x_hi[:, nb * P:(nb + 1) * P], x_lo[:, nb * P:(nb + 1) * P]
                        pairs = ((x_hi, wh), (x_hi, wl), (x_lo, wh))
                    else:
                        o = out_[:, 0:T]
                        wh, wl = wh[:, nb * P:(nb + 1) * P], wl[:, nb * P:(nb + 1) * P]
                        pairs = ((wh, x_hi), (wh, x_lo), (wl, x_hi))
                    for j, (l, r) in enumerate(pairs):
                        ins = pe.matmul(o, l, r, start=(s.k == 0 and i == 0 and not j),
                                        stop=(s.last and i == s.kts - 1 and j == 2))
                if s.last:
                    ins.then_inc(S("acc_ready"), 1)
                elif nb == NB - 1:
                    ins.then_inc(S("part_done"), 1)

            seen = [0]
            block_of = [(s_, nb_) for s_ in steps if s_.k == 0 for nb_ in range(NB)]

            def scan_slot(q):
                if q % 4 == 0 and q < HEADS:
                    g = q // 4
                    if g == 0:
                        pe.wait_ge(S("silu_done"), 32)
                    take("M3")
                    B, C = bct[:, g, :], bct[:, GROUPS + g, :]
                    pe.matmul(M3[:, 0:T], B[:, 0:P], C, start=True, stop=True)
                    pe.matmul(M3[:, T:T + P], B[:, P:T], C[:, P:T], start=True, stop=True).then_inc(S("scores"), 1)
                    free["M3"] = ("sc_done", g + 1)
                if q < HEADS:
                    bank = (M1, M2)[q % 2]
                    if q >= 2:
                        pe.wait_ge(S("seg_done"), q - 1)
                    pe.matmul(bank[:, 0:T], dta[:, 0, q:q + 1].to_broadcast([P, P]), tri[:, :], start=True, stop=False)
                    pe.matmul(bank[:, P:T], dta[:, 1, q:q + 1].to_broadcast([P, P]), tri[:, 0:P], start=False,
                              stop=True).then_inc(S("bc_done"), 1)
                h = q - 2
                if 0 <= h < HEADS:
                    o = HD * (h % 2)
                    pe.wait_ge(S("mul_done"), h + 1)
                    if h % 2 == 0:
                        take("M4")
                    pe.matmul(M4[o:o + HD, 0:T], xdt[:, 0, h * HD:(h + 1) * HD], ex[:, h % 2, 0:T], start=True,
                              stop=False)
                    pe.matmul(M4[o:o + HD, P:T], xdt[:, 1, h * HD:(h + 1) * HD], ex[:, h % 2, T:T + P], start=False,
                              stop=True).then_inc(S("y_done"), 1)
                    if h % 2:
                        free["M4"] = ("yadd_done", h // 2 + 1)

            def x_transpose(i):
                bank = ("M3", "M4")[i % 2]
                pe.wait_ge(S("silu_done"), 16 + i + 1)
                take(bank)
                b = (M3, M4)[i % 2]
                for t in range(TT):
                    ins = pe.transpose(b[:, t * P:(t + 1) * P], xs[:, i, t * P:(t + 1) * P], ident[:, :])
                ins.then_inc(S("xs_t"), 1)
                free[bank] = ("xdt_done", i + 1)

            def z_spread(g, name):
                take(name)
                pe.wait_ge(S("zroot"), g // 4 + 1)
                for t in range(TT):
                    ins = pe.matmul({"M3": M3, "M4": M4}[name][:, t * P:(t + 1) * P],
                                    zr[:, g, t:t + 1].to_broadcast([P, P]), ident[:, :], start=True, stop=True)
                ins.then_inc(S("zbc_done"), 1)
                free[name] = ("f_ready", YS + NB * (g + 1))

            def attn_tick(m):
                if m < 16:
                    bank = (M1, M2)[m % 2]
                    if m >= 2:
                        pe.wait_ge(S("l_done"), m - 1)
                    if m % 4 == 0:
                        pe.wait_ge(S("qk_done"), m + 4)
                    if m < 8:
                        qb, kb, o = m // 2, 4 + m // 2, HD * (m % 2)
                    else:
                        qb, kb, o = 8 + (m - 8) // 2, 12 + (m - 8) // 2, HD * (m % 2)
                    q, k = qk[o:o + HD, qb, :], qk[o:o + HD, kb, :]
                    fox = m >= 8
                    pe.matmul(bank[:, 0:P], q[:, 0:P], k[:, 0:P], start=True, stop=not fox)
                    if fox:
                        nl = [nlf[:, t, m - 8:m - 7].to_broadcast([P, P]) for t in range(TT)]
                        pe.wait_ge(S("nlf_done"), 1)
                        pe.matmul(bank[:, 0:P], nl[0], tri[:, 0:P], start=False, stop=True)
                    ins = pe.matmul(bank[:, P:3 * P], q[:, P:T], k, start=True, stop=not fox)
                    if fox:
                        pe.matmul(bank[:, P:3 * P], nl[0], tri[:, :], start=False, stop=False)
                        ins = pe.matmul(bank[:, 2 * P:3 * P], nl[1], tri[:, 0:P], start=False, stop=True)
                    ins.then_inc(S("s_done"), 1)
                c = product_of(m - 2)
                if c is not None:
                    w = m - 2
                    pe.wait_ge(S("diag_done"), w + 1)
                    take("M3")
                    pair = (w - 1, w) if c < 4 else (w,)
                    for i, t in enumerate((0, 1, 1)):
                        for w_ in pair:
                            ins = pe.matmul(M3[:, i * P:(i + 1) * P], EX[w_ % 4][:, i * P:(i + 1) * P],
                                            DIAG[w_ % 4][:, t * P:(t + 1) * P], start=(w_ == pair[0]), stop=(w_ == w))
                    ins.then_inc(S("tr_done"), 1)
                    free["M3"] = ("pt_done", c + 1)
                c = product_of(m - 3)
                if c is not None:
                    pe.wait_ge(S("pt_done"), c + 1)
                    pt = sc[:, c % 2, :]
                    pe.wait_ge(S("v_out"), NB * (c // 2 + 1 if c < 4 else 2 + c // 4))
                    if c < 4:
                        lo_, n_, o = 512 + c * P, P, 0
                    else:
                        lo_, n_, o = (c - 4) * HD, HD, HD * (c % 2)
                    if c < 4 or c % 2 == 0:
                        take("M4")
                    pe.matmul(M4[o:o + n_, 0:T], v[:, 0, lo_:lo_ + n_], pt[:, 0:T], start=True, stop=False)
                    pe.matmul(M4[o:o + n_, P:T], v[:, 1, lo_:lo_ + n_], pt[:, T:T + P], start=False, stop=True)\
                      .then_inc(S("pv_done"), 1)
                    if c < 4:
                        free["M4"] = ("o_copied", c + 1)
                    elif c % 2:
                        free["M4"] = ("f_ready", MX + 4 + (c - 4) // 2 + 1)
                c = product_of(m - 5)
                if c is not None and c < 4:
                    pe.wait_ge(S("osq"), c + 1)
                    take("M0")
                    pe.matmul(M0[:, 0:T], ones[:, :], sq[:, 0, :], start=True, stop=True).then_inc(S("osum"), 1)
                    free["M0"] = ("oroot", c + 1)

            def out_transpose(b):
                bank = ("M3", "M4")[b % 2]
                take(bank)
                pe.wait_ge(S("x_ready"), 5 * KB + b + 1)
                t_ = (M3, M4)[b % 2]
                for t in range(TT):
                    ins = pe.transpose(t_[:, t * P:(t + 1) * P], xT[:, b, t * P:(t + 1) * P], ident[:, :])
                ins.then_inc(S("otr_done"), 1)
                free[bank] = ("out_ready", b + 1)

            free["M0"] = ("mod_done", 2)
            jq = 0
            for n in range(NS):
                s = steps[n]
                for nb in range(NB):
                    product(n, nb)
                    if n == X0 + 2 and nb == 0:
                        pe.wait_ge(S("dta_done"), 1)
                        take("M3")
                        for t in range(TT):
                            o = M3[:, t * HEADS:(t + 1) * HEADS]
                            if t:
                                pe.matmul(o, ones[:, :], dta[:, 0, :], start=True, stop=False)
                            ins = pe.matmul(o, tri[:, 0:P], dta[:, t, :], start=(t == 0), stop=True)
                        ins.then_inc(S("ac_done"), 1)
                        free["M3"] = ("nac_done", 1)
                    zs = n - Z0
                    if 5 <= zs < 9 and nb == 0:
                        z_spread(zs - 5, "M4")
                    if zs == 9:
                        z_spread(4 + 2 * nb, "M4")
                        z_spread(5 + 2 * nb, "M3")
                    slot = NB * (n - X0) + nb
                    if 18 <= slot < 34:
                        x_transpose(slot - 18)
                    if 0 <= NB * (n - SCAN0) + nb < HEADS + 2:
                        scan_slot(NB * (n - SCAN0) + nb)
                    for kind, norm in (("wo", 1), ("o2", 4)):
                        if s.kind == kind and NB * s.j + nb:
                            x_sum(KB * norm + NB * s.j + nb - 1)
                    if s.kind == "dn" and s.k == 0 and s.j:
                        x_sum(KB * 2 + NB * (s.j - 1) + nb)
                    if nb == 0 and n and steps[n - 1].kind in ("dq", "dk", "fq", "fk"):
                        take("M0")
                        pe.wait_ge(S("qsq"), NB * (jq + 1))
                        for i in range(NB):
                            for t in range(TT):
                                c = 4 * i + 2 * t
                                ins = pe.matmul(M0[:, c:c + 2], sq[:, 2 + i, t * P:(t + 1) * P], blk64[:, 0:P:HD],
                                                start=True, stop=True)
                        jq += 1
                        ins.then_inc(S("qsum_done"), 1)
                        free["M0"] = ("qsum_read", jq)
                    if nb == 1 and n and steps[n - 1].kind in ("dq", "dk", "fq", "fk"):
                        pe.wait_ge(S("qr_ready"), jq)
                        take("M0")
                        for i in range(NB):
                            for t in range(TT):
                                c = 4 * i + 2 * t
                                ins = pe.matmul(M0[:, i * T + t * P:i * T + (t + 1) * P],
                                                rt[:, :, :].rearrange("p a b -> p (a b)")[:, c * HD:(c + 2) * HD], ident[:, :],
                                                start=True, stop=True)
                        ins.then_inc(S("qbc_done"), 1)
                        free["M0"] = ("qk_done", NB * jq)
                    if (n, nb) in tick_at:
                        attn_tick(tick_at[n, nb])
                    if s.kind == "d2" and s.k == 0 and s.j:
                        out_transpose(NB * (s.j - 1) + nb)
                    if s.kind == "fq" and s.j == 0 and nb == 1:
                        pe.wait_ge(S("nlf_done"), 1)
                        take("M0")
                        for t in range(TT):
                            o = M0[:, t * 8:(t + 1) * 8]
                            if t:
                                pe.matmul(o, ones[:, :], nlf[:, 0, :], start=True, stop=False)
                            ins = pe.matmul(o, tri[:, 0:P], nlf[:, t, :], start=(t == 0), stop=True)
                        ins.then_inc(S("fc_done"), 1)
                        free["M0"] = ("fcum_done", 1)
                zs = n - Z0
                if 1 <= zs < 9:
                    if zs in (1, 5):
                        take("M3")
                    pe.wait_ge(S("zsq"), NB * zs)
                    for t in range(TT):
                        c = TT * (zs - 1) + t
                        for i in range(NB):
                            ins = pe.matmul(M3[:, c:c + 1], sq[:, 2 * (zs % 2) + i, t * P:(t + 1) * P], ones[:, 0:1],
                                            start=(i == 0), stop=(i == 1))
                    ins.then_inc(S("zsum_done"), 1)
                    free["M3"] = ("zroot", 1 if zs < 5 else 2)
                if n - 2 in col_at:
                    ada_column(col_at[n - 2])
                if s.kind == "wo" and s.j == 3:
                    x_sum(2 * KB - 1)
                if s.kind == "dn" and s.j == 3 and s.last:
                    x_sum(3 * KB - 2)
                    x_sum(3 * KB - 1)
                    for b in range(KB):
                        x_sum(3 * KB + b)
                if s.kind == "fv" and s.j == 1:
                    for m in last_ticks:
                        attn_tick(m)
                if s.kind == "o2" and s.j == 3:
                    x_sum(5 * KB - 1)
            out_transpose(KB - 2)
            out_transpose(KB - 1)

        @block.vector
        def _(dve):
            chain = [0]

            def link(ins):
                chain[0] += 1
                ins.then_inc(S("dve_chain"), 1)
                dve.wait_ge(S("dve_chain"), chain[0])

            def split_lo(n):
                s = steps[n]
                dve.wait_ge(S("hi_ready"), n + 1)
                hi, lo = (w[:, n % NHL, 0:s.kts, 0:s.cols] for w in (w_hi, w_lo))
                dve.tensor_tensor(lo, raw_of(("step", n), s), hi.bitcast(F32), ALU.subtract).then_inc(S("lo_ready"), 1)

            def f_slot(i):
                if i >= NF:
                    dve.wait_ge(S("act_lo"), i - NF + 1)
                return fr[:, i % NF, :]

            def take_mod(c0, c1):
                if c1 <= NB * NA0:
                    dve.wait_ge(S("ada_used"), NA0)
                else:
                    dve.wait_ge(S("col_used"), c1 - NB * NA0)
                dve.tensor_tensor(mod[:, c0:c1], mod_bank(c0)[:, c0:c1], ada_b[:, c0:c1], ALU.add)\
                   .then_inc(S("mod_done"), 1)

            def make_gain(n):
                link(dve.scalar_tensor_tensor(gain[:, n, :], SCL[n], 1.0, LN[n], ALU.add, ALU.mult))

            def x_norm(n):
                dve.wait_ge(S("xroot"), n + 1)
                for b in range(KB):
                    if NORM_U[n] is None:
                        dve.scalar_tensor_tensor(xT[:, b, :], xT[:, b, :], final_w[:, b:b + 1], rt[:, 0, :], ALU.mult,
                                                 ALU.mult).then_inc(S("x_ready"), 1)
                    else:
                        i = NORM_U[n] + b
                        f = f_slot(i)
                        ins = dve.scalar_tensor_tensor(f, xT[:, b, :], gain[:, n, b:b + 1], rt[:, 0, :], ALU.mult,
                                                       ALU.mult)
                        if b % 2:
                            link(ins)
                            ins = dve.tensor_scalar(f, f, SH[n][:, b:b + 1], None, ALU.add)
                        ins.then_inc(S("f_ready"), 1)

            def softplus(w, z, k, sign):
                dve.wait_ge(S("sp_e"), k + 1)
                link(dve.tensor_scalar(w[:, 2, :], w[:, 1, :], 1.0, None, ALU.add))
                dve.tensor_scalar(w[:, 4, :], w[:, 2, :], -1.0, None, ALU.add).then_inc(S("sp_w"), 1)
                dve.wait_ge(S("sp_w"), k + 1)
                link(dve.tensor_tensor(w[:, 4, :], w[:, 1, :], w[:, 4, :], ALU.subtract))
                link(dve.reciprocal(w[:, 0, :], w[:, 2, :]))
                link(dve.tensor_tensor(w[:, 4, :], w[:, 4, :], w[:, 0, :], ALU.mult))
                dve.wait_ge(S("sp_ln"), k + 1)
                link(dve.tensor_tensor(w[:, 4, :], w[:, 4, :], w[:, 3, :], ALU.add))
                link(dve.tensor_scalar(w[:, 0, :], z, sign, 0.0, ALU.mult, ALU.max))
                link(dve.tensor_tensor(w[:, 4, :], w[:, 4, :], w[:, 0, :], ALU.add))

            def early_ada(n):
                dve.wait_ge(S("ada_mul_a"), n + 1)
                dve.wait_ge(S("ada_mul_b"), n + 1)
                if n >= 2:
                    dve.wait_ge(S("ada_used"), n - 1)
                dve.tensor_reduce(ada_sum[:, n % 2, :], raw_of(("ada", n)).rearrange("p k c -> p c k"), AX_X,
                                  ALU.add).then_inc(S("ada_sum"), 1)

            dve.wait_ge(S("pc"), N_CONST)
            dve.wait_ge(S("par_t"), 3)
            for i, bank in enumerate((M1, M2, M3)):
                ins = dve.tensor_copy(par[:, i, :], bank[:, 0:P])
            ins.then_inc(S("par_done"), 1)
            for b in range(KB):
                dve.wait_ge(S("xt_done"), b + 1)
                dve.tensor_copy(xT[:, b, :], (M1, M2, M3)[b % 3][:, 0:T]).then_inc(S("x_ready"), 1)
            for n in range(3):
                early_ada(n)
            dve.wait_ge(S("vec_in"), 16 * N_VEC)
            link(dve.tensor_tensor(lamw[:, 0, :], lamw[:, 0, :], lamw[:, 1, :], ALU.mult))
            link(dve.tensor_tensor(lamw[:, 2, :], lamw[:, 2, :], lamw[:, 3, :], ALU.mult))
            dve.tensor_reduce(small[:, 2:3], lamw[:, 0, :], AX_X, ALU.add)
            dve.tensor_reduce(small[:, 3:4], lamw[:, 2, :], AX_X, ALU.add).then_inc(S("lam_dots"), 1)
            dve.wait_ge(S("par_done"), 1)
            link(dve.tensor_scalar(small[:, 6:7], qk_gain[:, 0:1], HD ** -0.5, None, ALU.mult))
            link(dve.tensor_scalar(small[:, 7:8], qk_gain[:, 2:3], HD ** -0.5, None, ALU.mult))
            link(dve.tensor_scalar(small[:, 8:9], dn_gain, 1.0 - LAM_INIT, None, ALU.mult))
            dve.wait_ge(S("lam_exp"), 1)
            link(dve.tensor_tensor(small[:, 1:2], small[:, 5:6], small[:, 4:5], ALU.subtract))
            link(dve.tensor_scalar(small[:, 0:1], small[:, 1:2], -LAM_INIT, None, ALU.add))
            for half in range(2):
                link(dve.tensor_copy(dsk[half * HD:(half + 1) * HD, :], hb[half * HD:(half + 1) * HD, 2, half:HEADS:2]))
            dve.wait_ge(S("nega"), 1)
            link(dve.tensor_scalar(nega[:, :], nega[:, :], -1.0, None, ALU.mult))
            for n in range(3, NA0):
                early_ada(n)
            split_lo(0)
            take_mod(0, NB * NA0)
            dve.wait_ge(S("mod_done"), 1)
            make_gain(0)
            x_norm(0)
            split_lo(1)

            def seg_slot(q):
                if q < HEADS:
                    bank = (M1, M2)[q % 2]
                    dve.wait_ge(S("bc_done"), q + 1)
                    if q >= 2:
                        dve.wait_ge(S("exp_done"), q - 1)
                    dve.scalar_tensor_tensor(seg[:, q % 2, 0:T], bank[:, 0:T], nac[:, 0, q:q + 1], min_st[:, :],
                                             ALU.add, ALU.min)
                    dve.scalar_tensor_tensor(seg[:, q % 2, T:T + P], bank[:, P:T], nac[:, 1, q:q + 1], min_st[:, 0:P],
                                             ALU.add, ALU.min).then_inc(S("seg_done"), 1)
                if q >= 3 and q % 2:
                    p = (q - 3) // 2
                    dve.wait_ge(S("y_done"), 2 * p + 2)
                    dve.scalar_tensor_tensor(xs[:, p, :], xs[:, p, :], dsk[:, p:p + 1], M4[:, 0:T], ALU.mult,
                                             ALU.add).then_inc(S("yadd_done"), 1)

            def attn_tick(m):
                c = product_of(m - 6)
                if c is not None and c < 4:
                    dve.wait_ge(S("oroot"), c + 1)
                    dve.scalar_tensor_tensor(f_slot(MX + c), cv[:, c % 2, :], small[:, 8:9], sq[:, 1, :], ALU.mult,
                                             ALU.mult).then_inc(S("f_ready"), 1)
                w = m - 1
                if 0 <= w < 16:
                    r = rr[:, w % 4, :]
                    dve.wait_ge(S("ex_done"), w + 1)
                    if w >= 4:
                        dve.wait_ge(S("diag_done"), w - 3)
                    ins = dve.reciprocal(r, rs[:, w % 4, :])
                    if w < 8 and w % 2:
                        link(ins)
                        ins = dve.tensor_scalar(r, r, NEG_LAM, None, ALU.mult)
                    ins.then_inc(S("rr_ready"), 1)
                if m < 16:
                    b = m % 2
                    bank = (M1, M2)[b]
                    L = seg[:, b, :]
                    dve.wait_ge(S("s_done"), m + 1)
                    if m < 8:
                        slope = 2.0 ** (-8.0 * (m // 2 + 1) / 4)
                        link_l(dve.scalar_tensor_tensor(L, dist_ts[:, :], slope, bank[:, 0:3 * P], ALU.mult, ALU.add), m)
                    else:
                        f = m - 8
                        dve.scalar_tensor_tensor(L[:, 0:P], bank[:, 0:P], fcum[:, 0, f:f + 1], mask_ts[:, 0:P],
                                                 ALU.add, ALU.add)
                        link_l(dve.scalar_tensor_tensor(L[:, P:3 * P], bank[:, P:3 * P], fcum[:, 1, f:f + 1],
                                                        mask_ts[:, P:3 * P], ALU.add, ALU.add), m)
                    dve.tensor_reduce(nmx[:, b, 0:1], L[:, 0:P], AX_X, ALU.max, negate=True)
                    dve.tensor_reduce(nmx[:, b, 1:2], L[:, P:3 * P], AX_X, ALU.max, negate=True).then_inc(S("mx_done"), 1)
                c = product_of(m - 4)
                if c is not None and c < 4:
                    dve.wait_ge(S("pv_done"), c + 1)
                    dve.tensor_copy(cv[:, c % 2, :], M4[:, 0:T]).then_inc(S("o_copied"), 1)
                if c is not None and c >= 4 and c % 2:
                    dve.wait_ge(S("pv_done"), c + 1)
                    dve.tensor_copy(f_slot(MX + 4 + (c - 4) // 2), M4[:, 0:T]).then_inc(S("f_ready"), 1)

            def link_l(ins, m):
                ins.then_inc(S("l_done"), 1)
                dve.wait_ge(S("l_done"), m + 1)

            jq = 0
            for n in range(NS):
                s = steps[n]
                if n + 2 < NS and not split_late(n):
                    split_lo(n + 2)
                if n == MOD1_AT:
                    take_mod(NB * NA0, NB * NA0 + XCOL)
                    take_mod(NB * NA0 + XCOL, 48)
                    dve.wait_ge(S("mod_done"), 3)
                    make_gain(1)
                if n == MOD2_AT:
                    take_mod(48, 64)
                    dve.wait_ge(S("mod_done"), 4)
                    make_gain(3)
                if n == MOD3_AT:
                    take_mod(64, 88)
                    dve.wait_ge(S("mod_done"), 5)
                    make_gain(4)
                if n == MOD4_AT:
                    take_mod(88, 96)
                    dve.wait_ge(S("mod_done"), 6)
                for nb in range(NB):
                    bank = acc[(s.g + nb) % NACC]
                    ps, free = bank[:, 0:T], S(drained(s, nb)[0])
                    ready = lambda: dve.wait_ge(S("acc_ready"), s.g + nb + 1)
                    if s.kind == "dt":
                        ready()
                        dve.tensor_tensor(dtr[:, 0, nb * HEADS:(nb + 1) * HEADS], bank[:, 0:HEADS], hb[:, 0, :],
                                          ALU.add).then_inc(free, 1)
                    if s.kind == "fg":
                        ready()
                        dve.tensor_tensor(dtr[:, 0, nb * 8:(nb + 1) * 8], bank[:, 0:8], bf[:, :], ALU.add).then_inc(free, 1)
                    if s.kind == "xbc":
                        i = NB * s.j + nb
                        fb = (i + 16) % 32
                        dve.wait_ge(S("stg_ready"), i + 1)
                        dve.wait_ge(free, i + 1)
                        for tap in (2, 1, 0):
                            ins = dve.scalar_tensor_tensor(cv[:, i % 2, :], stg[:, i % 2, tap:tap + T],
                                                           ssm_w[:, 32 * tap + fb:32 * tap + fb + 1], cv[:, i % 2, :],
                                                           ALU.mult, ALU.add)
                            if tap:
                                link(ins)
                        ins.then_inc(S("conv_done"), 1)
                    slot = NB * (n - X0) + nb
                    if 18 <= slot < 34:
                        i = slot - 18
                        dve.wait_ge(S("xs_t"), i + 1)
                        dve.tensor_tensor(xdt[:, :, i * P:(i + 1) * P].rearrange("p t (h d) -> p t h d", d=HD),
                                          (M3, M4)[i % 2][:, 0:T].rearrange("p (t h d) -> p t h d", t=TT, d=HD),
                                          dt_sb[:, :, 2 * i:2 * i + 2].unsqueeze(3).to_broadcast([P, TT, 2, HD]),
                                          ALU.mult).then_inc(S("xdt_done"), 1)
                    if s.kind == "cx":
                        ready()
                        if s.j == 0 and nb == 0:
                            dve.wait_ge(S("silu_done"), 32)
                        b = NB * s.j + nb
                        dve.wait_ge(S("cc_out"), b + 1)
                        dve.tensor_tensor(stg[:, nb, 3:T + 3], ps, cct[:, nb, :], ALU.mult).then_inc(free, 1)
                        dve.wait_ge(free, b + 1)
                        link(dve.tensor_scalar(cv[:, nb, :], stg[:, nb, 3:T + 3], conv_w[:, 16 + b:17 + b], None, ALU.mult))
                        link(dve.scalar_tensor_tensor(cv[:, nb, :], stg[:, nb, 2:T + 2], conv_w[:, 8 + b:9 + b],
                                                      cv[:, nb, :], ALU.mult, ALU.add))
                        dve.scalar_tensor_tensor(cv[:, nb, :], stg[:, nb, 1:T + 1], conv_w[:, b:b + 1], cv[:, nb, :],
                                                 ALU.mult, ALU.add).then_inc(S("cx_done"), 1)
                    if s.kind == "cb":
                        ready()
                        i = YC + NB * s.j + nb
                        f = f_slot(i)
                        dve.wait_ge(S("cx_done"), NB * s.j + nb + 1)
                        dve.tensor_tensor(f, ps, cv[:, nb, :], ALU.mult).then_inc(S("f_ready"), 1)
                    if s.kind == "co":
                        ready()
                        dve.wait_ge(S("gate"), NB * s.j + nb + 1)
                        dve.tensor_tensor(mc[:, NB * s.j + nb, :], ps, gt[:, nb, :], ALU.mult).then_inc(S("gate_used"), 1)
                    if s.kind == "so" and s.last:
                        ready()
                        dve.wait_ge(S("gate"), 8 + NB * s.j + nb + 1)
                        dve.tensor_tensor(cv[:, nb, :], ps, gt[:, nb, :], ALU.mult).then_inc(S("gate_used"), 1)
                        dve.wait_ge(S("gate_used"), 8 + NB * s.j + nb + 1)
                        i = MG + NB * s.j + nb
                        dve.tensor_tensor(f_slot(i), cv[:, nb, :], mc[:, NB * s.j + nb, :], ALU.add)\
                           .then_inc(S("f_ready"), 1)
                    for kind, gate in (("wo", 0), ("dn", 1), ("o2", 2), ("d2", 3)):
                        if s.kind == kind and s.last:
                            ready()
                            b = NB * s.j + nb
                            dve.scalar_tensor_tensor(xT[:, b, :], ps, GATE[gate][:, b:b + 1], xT[:, b, :], ALU.mult,
                                                     ALU.add).then_inc(S("x_ready"), 1)
                    if s.kind == "up":
                        i = HID + NB * s.j + nb
                        dve.wait_ge(S("relu"), NB * s.j + nb + 1)
                        dve.tensor_tensor(f_slot(i), gt[:, nb, :], gt[:, nb, :], ALU.mult).then_inc(S("f_ready"), 1)
                    if s.kind == "u2":
                        i = HID2 + NB * s.j + nb
                        ready()
                        dve.wait_ge(S("silu_g"), NB * s.j + nb + 1)
                        dve.tensor_tensor(f_slot(i), ps, gt[:, nb, :], ALU.mult).then_inc(S("f_ready"), 1)
                    q = NB * (n - SCAN0) + nb
                    if 0 <= q < HEADS + 2:
                        seg_slot(q)
                    prev = steps[n - 1] if n else None
                    if nb == 1 and prev and prev.kind in ("dq", "dk", "fq", "fk"):
                        dve.wait_ge(S("qbc_done"), jq)
                        base, gcol = {"dq": (0, small[:, 7:8]), "dk": (4, qk_gain[:, 3:4]), "fq": (8, small[:, 6:7]),
                                      "fk": (12, qk_gain[:, 1:2])}[prev.kind]
                        for half in range(NB):
                            b = base + NB * prev.j + half
                            dve.scalar_tensor_tensor(qk[:, b, :], qk[:, b, :], gcol, M0[:, half * T:(half + 1) * T], ALU.mult, ALU.mult)\
                               .then_inc(S("qk_done"), 1)
                    if (n, nb) in tick_at:
                        attn_tick(tick_at[n, nb])
                    if nb == 0 and prev and prev.kind in ("dq", "dk", "fq", "fk"):
                        jq += 1
                        dve.wait_ge(S("qroot"), jq)
                        link(dve.scalar_tensor_tensor(qt[:, :], qs[:, :], HD * EPS, qr[:, :], ALU.add, ALU.mult))
                        link(dve.scalar_tensor_tensor(qt[:, :], qt[:, :], -0.5 / HD, qr[:, :], ALU.mult, ALU.mult))
                        wide = [t_[:, :].unsqueeze(2).to_broadcast([P, 8, HD]) for t_ in (qt, qr)]
                        dve.scalar_tensor_tensor(rt[:, :, :].rearrange("p a (b c) -> p (a b) c", c=HD), wide[0], 1.5,
                                                 wide[1], ALU.add, ALU.mult).then_inc(S("qr_ready"), 1)
                    if s.kind == "fq" and s.j == 0 and nb == 1:
                        dve.wait_ge(S("fc_done"), 1)
                        dve.tensor_scalar(fcum[:, :, :].rearrange("p a b -> p (a b)"), M0[:, 0:16], -1.0, None, ALU.mult)\
                           .then_inc(S("fcum_done"), 1)
                        dve.wait_ge(S("fcum_done"), 1)
                    if split_late(n) and nb == LO_NB:
                        split_lo(n + 2)
                    if n == X0 + 2 and nb == 0:
                        dve.wait_ge(S("ac_done"), 1)
                        dve.tensor_scalar(nac[:, :, :].rearrange("p a b -> p (a b)"), M3[:, 0:TT * HEADS], -1.0, None,
                                          ALU.mult).then_inc(S("nac_done"), 1)
                if s.kind == "dt":
                    softplus(dtr[:, 1:6, :], dtr[:, 0, :], 0, 1.0)
                    flat = lambda t_: t_[:, :, :].rearrange("p a b -> p (a b)")
                    link(dve.tensor_copy(flat(dt_sb), dtr[:, 5, :]))
                    dve.tensor_tensor(dta[:, :, :], dt_sb[:, :, :], nega[:, :].unsqueeze(1).to_broadcast([P, TT, HEADS]),
                                      ALU.mult).then_inc(S("dta_done"), 1)
                if s.kind == "fg":
                    softplus(dtr[:, 1:6, 0:16], dtr[:, 0, 0:16], 1, -1.0)
                    dve.tensor_copy(nlf[:, :, :].rearrange("p a b -> p (a b)"), dtr[:, 5, 0:16])\
                       .then_inc(S("nlf_done"), 1)
                zs = n - Z0
                for b in z_blocks(zs):
                    g = b // NB
                    bank = M3 if zs == 9 and g % 2 else M4
                    dve.wait_ge(S("zbc_done"), g + 1)
                    dve.scalar_tensor_tensor(f_slot(YS + b), xs[:, b, :], norm_w[:, b:b + 1], bank[:, 0:T], ALU.mult,
                                             ALU.mult).then_inc(S("f_ready"), 1)
                if n - 1 in col_at:
                    m = col_at[n - 1]
                    dve.wait_ge(S("col_mul"), m + 1)
                    if m >= 2:
                        dve.wait_ge(S("col_used"), m - 1)
                    dve.tensor_reduce(cols[:, m % 2, :], colw[:, m % 2, :, :].rearrange("p k c -> p c k"), AX_X,
                                      ALU.add).then_inc(S("col_sum"), 1)
                if s.kind == "wo" and s.j == 3:
                    x_norm(1)
                if s.kind == "dn" and s.j == 3 and s.last:
                    x_norm(2)
                    x_norm(3)
                if s.kind == "fv" and s.j == 1:
                    for m in last_ticks:
                        attn_tick(m)
                if s.kind == "o2" and s.j == 3:
                    x_norm(4)


_INS = ["x", "c", "w_ada", "b_ada", "ln1", "ln2", "w_in", "conv_w", "ssm_conv_w", "ssm_conv_b", "dt_bias", "a_log",
        "d_skip", "ssm_norm_w", "w_conv_out", "w_ssm_out", "w_o", "w_up", "w_down", "final_norm", "c_2", "ln1_g_2",
        "ln2_g_2", "w_ada_2", "b_ada_2", "w_in_2", "b_f_2", "fox_qk_g_2", "diff_qk_g_2", "diff_lam_2", "diff_norm_g_2",
        "w_out_2", "w_gate_2", "w_up_2", "w_down_2"]


def kernel(**inputs):
    import numpy as _np
    import concourse.bacc as _bacc
    from concourse import mybir as _mybir
    from concourse.bass_utils import run_bass_kernel_spmd as _run

    nc = _bacc.Bacc("TRN2", target_bir_lowering=False, num_devices=1)
    arrays, args = {}, {}
    for name in _INS:
        x = _np.ascontiguousarray(inputs[name])
        arrays[f"in_{name}"] = x
        args[name] = nc.dram_tensor(f"in_{name}", x.shape, _mybir.dt.from_np(x.dtype), kind="ExternalInput").ap()
    out = nc.dram_tensor("out", (1, T, D), F32, kind="ExternalOutput").ap()
    build(nc, args, out)
    r = _run(nc, [arrays], core_ids=[0])
    return r.results[0]["out"]
```
